# Optimizing a Trainium2 kernel written in Bass

```python
import math
import jax, jax.numpy as jnp
from jax import lax
import numpy as np

D_MODEL = 1024
BATCH = 1
SEQ = 256
DEPTH = 1

HEAD_DIM = 64
N_HEADS_MOBA = 8
N_HEADS_FOX = 8
MOBA_WIDTH = N_HEADS_MOBA * HEAD_DIM
FOX_WIDTH = N_HEADS_FOX * HEAD_DIM
MIX_WIDTH = MOBA_WIDTH + FOX_WIDTH
IN_WIDTH = 3 * MOBA_WIDTH + 3 * FOX_WIDTH + N_HEADS_FOX
MOBA_BLOCK = 256
MOBA_TOPK = 3
MOBA_QCHUNK = 64
FOX_QBLOCK = 128
N_BUCKETS = 32
MAX_DISTANCE = 128
N_MEM = 256
XATTN_HEADS = 4
XATTN_HEAD_DIM = D_MODEL // XATTN_HEADS
PEER_HEADS = 8
PEER_NKEYS = 128
PEER_N_EXPERTS = PEER_NKEYS * PEER_NKEYS
PEER_TOPK = 16
PEER_DKEY = 128
PEER_TOKEN_CHUNK = 128
EPS = 1e-6
NEG_INF = -1e30

kernel_name = "hymba_moba_fox_peer_layer"

def rmsnorm(x, g):
    xf = x.astype(jnp.float32)
    y = xf * lax.rsqrt(jnp.mean(xf * xf, axis=-1, keepdims=True) + EPS)
    return (y * g.astype(jnp.float32)).astype(x.dtype)

def t5_bucket(dist):
    max_exact = N_BUCKETS // 2
    d = jnp.maximum(dist, 0)
    df = jnp.maximum(d, 1).astype(jnp.float32)
    large = max_exact + (jnp.log(df / max_exact) / math.log(MAX_DISTANCE / max_exact)
                         * (N_BUCKETS - max_exact)).astype(jnp.int32)
    large = jnp.minimum(large, N_BUCKETS - 1)
    return jnp.where(d < max_exact, d, large)

def moba_attention(q, k, v, rel_bias):
    B, S, H, Dh = q.shape
    scale = Dh ** -0.5
    pad = (-S) % MOBA_BLOCK
    kp = jnp.pad(k, ((0, 0), (0, pad), (0, 0), (0, 0)))
    vp = jnp.pad(v, ((0, 0), (0, pad), (0, 0), (0, 0)))
    nblk = (S + pad) // MOBA_BLOCK
    kk = min(MOBA_TOPK, nblk)
    kh = kp.reshape(B, nblk, MOBA_BLOCK, H, Dh).transpose(0, 3, 1, 2, 4)
    vh = vp.reshape(B, nblk, MOBA_BLOCK, H, Dh).transpose(0, 3, 1, 2, 4)
    kmean = jnp.mean(kh.astype(jnp.float32), axis=3).astype(q.dtype)
    nq = S // MOBA_QCHUNK
    qc = q.reshape(B * nq, MOBA_QCHUNK, H, Dh)
    b_idx = jnp.repeat(jnp.arange(B, dtype=jnp.int32), nq)
    c_idx = jnp.tile(jnp.arange(nq, dtype=jnp.int32), B)
    head_ix = jnp.arange(H)
    offs = jnp.arange(MOBA_BLOCK, dtype=jnp.int32)
    blk = jnp.arange(nblk, dtype=jnp.int32)

    def one_chunk(args):
        qb, b, c = args
        kb, vb, km = kh[b], vh[b], kmean[b]
        t = c * MOBA_QCHUNK + jnp.arange(MOBA_QCHUNK, dtype=jnp.int32)
        i = (c * MOBA_QCHUNK) // MOBA_BLOCK
        bs = jnp.einsum('qhd,hnd->qhn', qb, km).astype(jnp.float32)
        bs = jnp.where(blk[None, None, :] < i, bs, NEG_INF)
        _, sel = lax.top_k(bs, kk)
        sel_valid = jnp.arange(kk)[None, None, :] < i
        ks = kb[head_ix[None, :, None], sel]
        vs = vb[head_ix[None, :, None], sel]
        s_sel = jnp.einsum('qhd,qhrld->qhrl', qb, ks).astype(jnp.float32) * scale
        kpos_sel = sel[..., None] * MOBA_BLOCK + offs
        bias_sel = rel_bias[t5_bucket(t[:, None, None, None] - kpos_sel),
                            head_ix[None, :, None, None]].astype(jnp.float32)
        s_sel = jnp.where(sel_valid[..., None], s_sel + bias_sel, NEG_INF)
        ko = lax.dynamic_index_in_dim(kb, i, axis=1, keepdims=False)
        vo = lax.dynamic_index_in_dim(vb, i, axis=1, keepdims=False)
        s_own = jnp.einsum('qhd,hld->qhl', qb, ko).astype(jnp.float32) * scale
        dist_own = t[:, None] - (i * MOBA_BLOCK + offs)[None, :]
        bias_own = rel_bias[t5_bucket(dist_own)].astype(jnp.float32).transpose(0, 2, 1)
        s_own = jnp.where((dist_own >= 0)[:, None, :], s_own + bias_own, NEG_INF)
        qn = qb.shape[0]
        logits = jnp.concatenate([s_sel.reshape(qn, H, kk * MOBA_BLOCK), s_own], axis=-1)
        p = jax.nn.softmax(logits, axis=-1).astype(v.dtype)
        p_sel = p[..., :kk * MOBA_BLOCK].reshape(qn, H, kk, MOBA_BLOCK)
        p_own = p[..., kk * MOBA_BLOCK:]
        return (jnp.einsum('qhrl,qhrld->qhd', p_sel, vs)
                + jnp.einsum('qhl,hld->qhd', p_own, vo))

    out = lax.map(one_chunk, (qc, b_idx, c_idx))
    return out.reshape(B, S, H, Dh)

def forgetting_attention(q, k, v, f_logit):
    B, S, H, Dh = q.shape
    scale = Dh ** -0.5
    c = jnp.cumsum(jax.nn.log_sigmoid(f_logit.astype(jnp.float32)), axis=1)
    cT = c.transpose(0, 2, 1)
    nqb = S // FOX_QBLOCK
    qb = q.reshape(B, nqb, FOX_QBLOCK, H, Dh).transpose(1, 0, 2, 3, 4)
    cb = c.reshape(B, nqb, FOX_QBLOCK, H).transpose(1, 0, 3, 2)
    kpos = jnp.arange(S, dtype=jnp.int32)

    def one_block(args):
        qq, cq, j = args
        s = jnp.einsum('bqhd,bkhd->bhqk', qq, k).astype(jnp.float32) * scale
        decay = cq[..., None] - cT[:, :, None, :]
        tpos = j * FOX_QBLOCK + jnp.arange(FOX_QBLOCK, dtype=jnp.int32)
        mask = kpos[None, :] <= tpos[:, None]
        s = jnp.where(mask, s + decay, NEG_INF)
        p = jax.nn.softmax(s, axis=-1).astype(v.dtype)
        return jnp.einsum('bhqk,bkhd->bqhd', p, v)

    out = lax.map(one_block, (qb, cb, jnp.arange(nqb, dtype=jnp.int32)))
    return out.transpose(1, 0, 2, 3, 4).reshape(B, S, H, Dh)

def hybrid_mixer(h, w_in, b_forget, rel_bias, g_moba_out, g_fox_out, w_out):
    B, S, _ = h.shape
    proj = h @ w_in
    cuts = np.cumsum([MOBA_WIDTH] * 3 + [FOX_WIDTH] * 3).tolist()
    qm, km, vm, qf, kf, vf, fl = jnp.split(proj, cuts, axis=-1)
    hd = lambda a, n: a.reshape(B, S, n, HEAD_DIM)
    o_a = moba_attention(hd(qm, N_HEADS_MOBA), hd(km, N_HEADS_MOBA), hd(vm, N_HEADS_MOBA), rel_bias)
    o_b = forgetting_attention(hd(qf, N_HEADS_FOX), hd(kf, N_HEADS_FOX), hd(vf, N_HEADS_FOX),
                               fl + b_forget)
    o = jnp.concatenate([rmsnorm(o_a.reshape(B, S, MOBA_WIDTH), g_moba_out),
                         rmsnorm(o_b.reshape(B, S, FOX_WIDTH), g_fox_out)], axis=-1)
    return o @ w_out

def memory_cross_attention(h, mem_n, w_q, w_k, w_v, w_o):
    B, S, _ = h.shape
    M = mem_n.shape[1]
    q = (h @ w_q).reshape(B, S, XATTN_HEADS, XATTN_HEAD_DIM)
    k = (mem_n @ w_k).reshape(B, M, XATTN_HEADS, XATTN_HEAD_DIM)
    v = (mem_n @ w_v).reshape(B, M, XATTN_HEADS, XATTN_HEAD_DIM)
    s = jnp.einsum('bshd,bmhd->bhsm', q, k).astype(jnp.float32) * XATTN_HEAD_DIM ** -0.5
    p = jax.nn.softmax(s, axis=-1).astype(v.dtype)
    o = jnp.einsum('bhsm,bmhd->bshd', p, v).reshape(B, S, D_MODEL)
    return o @ w_o

def peer_ffn(h, w_query, sub_keys_1, sub_keys_2, expert_down, expert_up):
    B, S, D = h.shape
    T = B * S
    hc = h.reshape(T // PEER_TOKEN_CHUNK, PEER_TOKEN_CHUNK, D)
    half = PEER_DKEY // 2

    def one_chunk(xc):
        C = xc.shape[0]
        qr = (xc @ w_query).reshape(C, PEER_HEADS, 2, half)
        s1 = jnp.einsum('chd,hnd->chn', qr[:, :, 0], sub_keys_1).astype(jnp.float32)
        s2 = jnp.einsum('chd,hnd->chn', qr[:, :, 1], sub_keys_2).astype(jnp.float32)
        v1, i1 = lax.top_k(s1, PEER_TOPK)
        v2, i2 = lax.top_k(s2, PEER_TOPK)
        cand = (v1[..., :, None] + v2[..., None, :]).reshape(C, PEER_HEADS, PEER_TOPK * PEER_TOPK)
        cand_idx = (i1[..., :, None] * PEER_NKEYS + i2[..., None, :]).reshape(
            C, PEER_HEADS, PEER_TOPK * PEER_TOPK)
        top_s, pos = lax.top_k(cand, PEER_TOPK)
        eidx = jnp.take_along_axis(cand_idx, pos, axis=-1)
        g = jax.nn.softmax(top_s, axis=-1)
        u = expert_down[eidx]
        a = jax.nn.gelu(jnp.einsum('cd,chkd->chk', xc, u).astype(jnp.float32), approximate=False)
        vv = expert_up[eidx]
        return jnp.einsum('chk,chkd->cd', (g * a).astype(vv.dtype), vv)

    return lax.map(one_chunk, hc).reshape(B, S, D)

def setup_inputs(seed: int = 0) -> dict:
    key = jax.random.key(seed)
    ks = jax.random.split(key, 24)
    nrm = lambda k, shape, s: jax.random.normal(k, shape, jnp.float32) * s
    gain = lambda k, shape: 1.0 + 0.01 * jax.random.normal(k, shape, jnp.float32)
    L = DEPTH
    return {
        "x": nrm(ks[0], (BATCH, SEQ, D_MODEL), 1.0),
        "mem": nrm(ks[1], (BATCH, N_MEM, D_MODEL), 1.0),
        "norm_mix": gain(ks[2], (L, D_MODEL)),
        "w_in": nrm(ks[3], (L, D_MODEL, IN_WIDTH), D_MODEL ** -0.5),
        "b_forget": 2.0 + 0.1 * jax.random.normal(ks[4], (L, N_HEADS_FOX), jnp.float32),
        "rel_bias": nrm(ks[5], (N_BUCKETS, N_HEADS_MOBA), 0.5),
        "g_moba_out": gain(ks[6], (L, MOBA_WIDTH)),
        "g_fox_out": gain(ks[7], (L, FOX_WIDTH)),
        "w_out": nrm(ks[8], (L, MIX_WIDTH, D_MODEL), MIX_WIDTH ** -0.5),
        "norm_xattn": gain(ks[9], (L, D_MODEL)),
        "norm_mem": gain(ks[10], (L, D_MODEL)),
        "w_xq": nrm(ks[11], (L, D_MODEL, D_MODEL), D_MODEL ** -0.5),
        "w_xk": nrm(ks[12], (L, D_MODEL, D_MODEL), D_MODEL ** -0.5),
        "w_xv": nrm(ks[13], (L, D_MODEL, D_MODEL), D_MODEL ** -0.5),
        "w_xo": nrm(ks[14], (L, D_MODEL, D_MODEL), D_MODEL ** -0.5),
        "norm_ffn": gain(ks[15], (L, D_MODEL)),
        "w_peer_query": nrm(ks[16], (L, D_MODEL, PEER_HEADS * PEER_DKEY), D_MODEL ** -0.5),
        "peer_subkeys_1": nrm(ks[17], (L, PEER_HEADS, PEER_NKEYS, PEER_DKEY // 2), (PEER_DKEY // 2) ** -0.5),
        "peer_subkeys_2": nrm(ks[18], (L, PEER_HEADS, PEER_NKEYS, PEER_DKEY // 2), (PEER_DKEY // 2) ** -0.5),
        "peer_expert_down": nrm(ks[19], (L, PEER_N_EXPERTS, D_MODEL), D_MODEL ** -0.5),
        "peer_expert_up": nrm(ks[20], (L, PEER_N_EXPERTS, D_MODEL), PEER_HEADS ** -0.5),
        "norm_final": gain(ks[21], (D_MODEL,)),
    }

def reference(x, mem, norm_mix, w_in, b_forget, rel_bias, g_moba_out, g_fox_out, w_out,
              norm_xattn, norm_mem, w_xq, w_xk, w_xv, w_xo, norm_ffn, w_peer_query,
              peer_subkeys_1, peer_subkeys_2, peer_expert_down, peer_expert_up, norm_final):
    for l in range(DEPTH):
        h = rmsnorm(x, norm_mix[l])
        x = x + hybrid_mixer(h, w_in[l], b_forget[l], rel_bias, g_moba_out[l], g_fox_out[l], w_out[l])
        h = rmsnorm(x, norm_xattn[l])
        mem_n = rmsnorm(mem, norm_mem[l])
        x = x + memory_cross_attention(h, mem_n, w_xq[l], w_xk[l], w_xv[l], w_xo[l])
        h = rmsnorm(x, norm_ffn[l])
        x = x + peer_ffn(h, w_peer_query[l], peer_subkeys_1[l], peer_subkeys_2[l],
                         peer_expert_down[l], peer_expert_up[l])
    return rmsnorm(x, norm_final)


_drawn_inputs = setup_inputs


def setup_inputs(seed=0):
    import zlib

    import numpy as np

    out = dict(_drawn_inputs(seed))
    spreads = {}
    factors = {'norm_mix': 3.129,
     'g_moba_out': 5.164,
     'g_fox_out': 5.415,
     'norm_xattn': 8.0,
     'norm_mem': 8.0,
     'norm_ffn': 35.944,
     'norm_final': 30.019}
    for name, (base, spread) in spreads.items():
        noise = np.random.default_rng([zlib.crc32(name.encode()), seed]).standard_normal(out[name].shape)
        drawn = base * np.exp(spread * noise) if base else spread * noise
        out[name] = __import__('jax').numpy.asarray(drawn.astype(out[name].dtype))
    for name, factor in factors.items():
        out[name] = (out[name] * factor).astype(out[name].dtype)
    return out
```

```python
import math
from contextlib import ExitStack

import numpy as np
import concourse.bass as bass
from concourse import mybir

P = 128
D = 1024
SEQ = 256
T = SEQ // P
M = 256
KC = D // P
HD = 64
NH = 8
BLK = 512
XH_N, XHD = 4, 256
PH, PK = 8, 16
NKEY = 128
N_BUCKETS, MAX_DISTANCE = 32, 128
EPS = 1e-6
NEG = -1e30
W_SLOTS = 7
U = 4
GPH = PK // U
GPT = PH * GPH
FDIST = 384


def bucket_rows():
    max_exact = N_BUCKETS // 2
    rows = np.zeros((N_BUCKETS + 1, FDIST), np.float32)
    for m in range(FDIST):
        d = (SEQ - 1) - m
        if d < 0:
            rows[N_BUCKETS, m] = NEG
            continue
        b = d
        if d >= max_exact:
            b = min(max_exact + int(math.log(d / max_exact) / math.log(MAX_DISTANCE / max_exact)
                                    * (N_BUCKETS - max_exact)), N_BUCKETS - 1)
        rows[b, m] = 1.0
    return rows


def hybrid_layer(nc, A, out, bias_scratch):
    f32, i32, u32 = mybir.dt.float32, mybir.dt.int32, mybir.dt.uint32
    ALU, ACT, AX = mybir.AluOpType, mybir.ActivationFunctionType, mybir.AxisListType

    down_rows = A["peer_expert_down"].rearrange("l e d -> (l e) d")
    up_rows = A["peer_expert_up"].rearrange("l e d -> (l e) d")

    blocks = []
    for name, cols in (("w_xk", 2), ("w_xv", 2), ("w_in", 6), ("w_out", 2), ("w_xq", 2), ("w_xo", 2),
                       ("w_peer_query", 2)):
        blocks += [(name, b) for b in range(cols)]
    BN = {key: n for n, key in enumerate(blocks)}

    def chain_x(t):
        v = [("xT", t, 0), ("xT", t, 1)] + [("xO", t, h) for h in range(XH_N)]
        v += [("xo", t, 0), ("xo", t, 1)]
        a = [("xq", t, 0), ("xq", t, 1)]
        for h in range(XH_N):
            a += [("xS", t, h), ("xPT", t, h)]
        return v, a

    v_jobs = [("gains",)] + [("skT", i) for i in range(2)]
    v_jobs += [("memT", m, i) for m in range(2) for i in range(2)]
    v_jobs += [("hT", t, i) for t in range(T) for i in range(2)]
    v_jobs += [("forget",)]
    a_jobs = [("bias",)] + [("mK", b, i) for b in range(2) for i in range(2)]
    a_jobs += [("mV", b, m) for b in range(2) for m in range(2)]
    for b in range(6):
        v_jobs += [("win", b, 0)]
        a_jobs += [("win", b, 1)]
    for t in range(T):
        v_jobs += [("S", t, h) for h in range(2 * NH)]
        a_jobs += [("PT", t, h) for h in range(2 * NH)]
    for t in range(T):
        v_jobs += [("oT", t, 0), ("oT", t, 1), ("wout", t, 0), ("wout", t, 1)]
    for t in range(T):
        v, a = chain_x(t)
        v_jobs += v + [("pT", t, 0), ("pT", t, 1)]
        a_jobs += a + [("wq", t, 0), ("wq", t, 1)] + [("sc", t, i) for i in range(4)]
    VN = {key: n for n, key in enumerate(v_jobs)}
    AN = {key: n for n, key in enumerate(a_jobs)}

    ctx = ExitStack()
    with ctx:
        def sb(name, shape, dt=f32):
            return ctx.enter_context(nc.sbuf_tensor(name, shape, dt))

        def pb(name, shape, dt=f32):
            return ctx.enter_context(nc.psum_tensor(name, shape, dt))

        def sem(name):
            return ctx.enter_context(nc.semaphore(name))

        W = sb("weights", [P, W_SLOTS, KC * BLK])
        QKVB = sb("qkvb", [P, 8, D])
        Q = QKVB[:, 0:2, :].rearrange("p t (c x) -> p t c x", c=KC)
        K = QKVB[:, 2:4, :].rearrange("p t (c x) -> p t c x", c=KC)
        V = QKVB[:, 4:6, :]
        B = QKVB[:, 6:8, :].rearrange("p a (h x) -> p (a h) x", h=4)
        XH = sb("x_and_h", [P, T, 2, D])
        X = [XH[:, t, 0, :] for t in range(T)]
        HTpage = [XH[:, t, 1, :] for t in range(T)]
        HT = [h.rearrange("p (c x) -> p c x", c=KC) for h in HTpage]
        KM = sb("mem_k", [P, KC, M])
        VM = sb("mem_v", [P, 2, D])
        XS = sb("scaled", [P, D])
        XQ = XS[:, :].rearrange("p (c x) -> p c x", c=KC)
        gffn = sb("gffn", [P, D])
        ident = sb("ident", [P, P])
        FM = sb("fox_mask", [P, SEQ])
        Ssb = sb("s_sb", [P, 2, SEQ])
        Pr = sb("probs", [P, 2, SEQ])
        PT = sb("probs_t", [P, 2, SEQ])
        skT = sb("subkeys_t", [P, PH, NKEY])
        grow = sb("gain_rows", [32, P])
        gcol = sb("gain_cols", [P, 32])
        wf = sb("w_forget", [P, KC, NH])
        bf = sb("b_forget_col", [NH, 1])
        relb = sb("rel_rows", [N_BUCKETS + 1, NH])
        stat = sb("stat", [P, 16])
        eps = sb("eps", [P, 1])
        nmx = sb("neg_max", [P, 2])
        rsum = sb("row_sum", [P, 2 * NH])
        rinv = sb("row_inv", [P, 2 * NH])
        xsum = sb("x_sum", [P, 2])
        xinv = sb("x_inv", [P, 2])
        kv = sb("key_vals", [P, 2, PK])
        ku = sb("key_idx", [P, 2, PK], u32)
        kf = sb("key_idx_f", [P, 2, PK])
        tv = sb("top_vals", [P, PK])
        pos = sb("top_pos", [P, PK], u32)
        pab = sb("pos_ab", [P, 2, PK], u32)
        pabf = sb("pos_ab_f", [P, 2, PK])
        hot = sb("one_hot", [P, 2, PK, PK])
        iota16 = sb("iota16", [P, PK])
        picked = sb("picked", [P, 2, PK])
        tneg = sb("top_neg", [P, 1])
        texp = sb("top_exp", [P, PK])
        tsum = sb("top_sum", [P, 1])
        tinv = sb("top_inv", [P, 1])
        IDX = sb("expert_idx", [P, 2, PK])
        GATE = sb("gates", [P, 2, PK])
        ixd = sb("ix_down", [P, 2, U], i32)
        ixu = sb("ix_up", [P, 2, U], i32)
        dots = sb("dots", [P, 2, U])
        gel = sb("gelu", [P, 2, U])
        wgt = sb("wgt", [P, 2, U])
        diag = sb("diag", [P, 2, U, P])
        small = diag[0:NH, :, :, :].rearrange("p a (u b) x -> p (a u) (b x)", b=2)
        cand = Ssb[:, 0, :]
        sc = Ssb[:, 1, :].rearrange("p (a x) -> p a x", a=2)

        DN = [QKVB[:, i, :] for i in range(U)]
        free_slot = BN[("w_out", 1)] % W_SLOTS
        UPB = [QKVB[:, 4 + i, :] for i in range(U)]
        UPB += [W[:, free_slot, i * D:(i + 1) * D] for i in range(U)]

        def wslot(name, b):
            return BN[(name, b)] % W_SLOTS

        def wblk(name, b):
            return W[:, wslot(name, b), :].rearrange("p (k c) -> p k c", k=KC)

        SALL = [XH[:, 0, :, :].rearrange("p a x -> p (a x)"), W[:, wslot("w_xq", 1), 0:2 * D]]
        QR = [W[:, free_slot, 0:D].rearrange("p (h x) -> p h x", h=PH),
              W[:, wslot("w_xq", 0), 0:D].rearrange("p (h x) -> p h x", h=PH)]
        gfin = W[:, wslot("w_xo", 0), 0:D]
        sk_nat = gffn[:, :].rearrange("p (h x) -> p h x", h=PH)
        sel = XS
        brow = Pr[0:NH, :, :].rearrange("p a x -> p (a x)")[:, 0:FDIST]
        onehot = Ssb[0:N_BUCKETS + 1, :, :].rearrange("p a x -> p (a x)")[:, 0:FDIST]
        YS = X

        vb = [pb(f"v_bank{i}", [P, BLK]) for i in range(2)]
        ab = [pb(f"a_bank{i}", [P, BLK]) for i in range(2)]
        y = pb("y", [P, D])
        hp = pb("h_psum", [P, D])

        v_full, v_free = sem("v_full"), sem("v_free")
        a_full, a_free = sem("a_full"), sem("a_free")
        ld_x = [sem(f"ld_x{t}") for t in range(T)]
        ld_mem = sem("ld_mem")
        ld_gain, ld_sk, ld_rel, ld_wf, ld_gffn, ld_gfin = (sem("ld_gain"), sem("ld_sk"), sem("ld_rel"),
                                                           sem("ld_wf"), sem("ld_gffn"), sem("ld_gfin"))
        w_full = [sem(f"w_full{i}") for i in range(W_SLOTS)]
        id_ready, fm_ready, rel_one, sel_ready, io_ready = (sem("id_ready"), sem("fm_ready"), sem("rel_one"),
                                                            sem("sel_ready"), sem("io_ready"))
        pool_ch, eps_ready = sem("pool_ch"), sem("eps_ready")
        sum_done = sem("sum_done")
        sq_done = sem("sq_done")
        xs_done = sem("xs_done")
        brow_out, ld_bias = sem("brow_out"), sem("ld_bias")
        fz, fe, fe1, fl, nc_ready = sem("fz"), sem("fe"), sem("fe1"), sem("fl"), sem("nc_ready")
        p_ready, o_full = sem("p_ready"), sem("o_full")
        o_raw = sem("o_raw")
        xmax, xp = sem("xmax"), sem("xp")
        top_in, top_exp, idx_ready = sem("top_in"), sem("top_e"), sem("idx_ready")
        go_dn = [sem(f"go_dn{i}") for i in range(2)]
        go_up = [sem(f"go_up{i}") for i in range(2)]
        dn_in = [sem(f"dn_in{i}") for i in range(U)]
        up_in = [sem(f"up_in{i}") for i in range(2 * U)]
        dot_done, gelu_done, diag_done, up_used = (sem("dot_done"), sem("gelu_done"), sem("diag_done"),
                                                   sem("up_used"))
        dve_ch = sem("dve_ch")
        w_done, hp_ready, top_ch = sem("w_done"), sem("hp_ready"), sem("top_ch")
        y_out, out_ready, out_done = sem("y_out"), sem("out_ready"), sem("out_done")

        norms = [("mem", 0), ("mem", 1), ("x", 0), ("x", 1), ("oA", 0), ("oB", 0), ("oA", 1), ("oB", 1),
                 ("xa", 0), ("pe", 0), ("xa", 1), ("pe", 1), ("fin", 0), ("fin", 1)]
        SQ = {key: n + 1 for n, key in enumerate(norms)}
        scaled = ["mem0", "mem1", "x0", "x1", "o0", "o1", "xa0", "pe0", "xa1", "pe1"]
        XN = {key: n + 1 for n, key in enumerate(scaled)}
        MEM = [Q[:, m, :, :].rearrange("p c x -> p (c x)") for m in range(2)]
        MEMT = [K[:, m, :, :] for m in range(2)]
        SC = {"mem0": MEM[0], "mem1": MEM[1], "x0": V[:, 0, :], "x1": V[:, 1, :], "o0": HTpage[0],
              "o1": HTpage[1], "xa0": XS[:, :], "xa1": XS[:, :], "pe0": XS[:, :], "pe1": XS[:, :]}

        CHAIN = ["norm_x", "xq0", "xq1", "h0", "h1", "h2", "h3", "xo0", "xo1", "norm_p", "wq0", "wq1", "sc"]
        AFTER = {2 * k + 1: piece for k, piece in enumerate(CHAIN)}
        assert 2 * len(CHAIN) - 1 < GPT - GPH

        block = ctx.enter_context(nc.Block())

        @block.sync
        def _(sp):
            def used_up(name, b):
                if name == "w_out":
                    return v_full, VN[("wout", 1, b)] + 1
                return a_full, AN[({"w_xk": "mK", "w_xv": "mV", "w_in": "win"}[name], b, 1)[:3]] + 1

            def load_block(n):
                name, b = blocks[n]
                if n >= W_SLOTS:
                    sp.wait_ge(*used_up(*blocks[n - W_SLOTS]))
                src = A[name][0].rearrange("(k p) c -> p k c", p=P)[:, :, b * BLK:(b + 1) * BLK]
                sp.dma_start(W[:, n % W_SLOTS, :].rearrange("p (k c) -> p k c", k=KC), src)\
                    .then_inc(w_full[n % W_SLOTS], 16)

            sp.dma_start(QKVB[:, 0:2, :], A["mem"][0].rearrange("(m p) d -> p m d", p=P)).then_inc(ld_mem, 16)
            for n in range(W_SLOTS):
                load_block(n)
                if n == 1:
                    for t in range(T):
                        sp.dma_start(X[t], A["x"][0, t * P:(t + 1) * P, :]).then_inc(ld_x[t], 16)
            sp.wait_ge(a_free, AN[("bias",)] + 1)
            sp.dma_start(bias_scratch, brow.unsqueeze(1).broadcast_to([NH, P, FDIST])).then_inc(brow_out, 16)
            sp.wait_ge(brow_out, 16)
            for h in range(NH):
                toeplitz = bass.AP(tensor=bias_scratch.tensor, offset=h * P * FDIST + P - 1,
                                   ap=[[FDIST - 1, P], [1, SEQ]])
                sp.dma_start(B[:, h, :], toeplitz).then_inc(ld_bias, 16)
            for n in range(W_SLOTS, len(blocks)):
                load_block(n)
                if blocks[n] == ("w_in", 5):
                    sp.wait_ge(v_free, VN[("skT", 1)] + 1)
                    sp.dma_start(gffn[:, :], A["norm_ffn"][0:1, :].broadcast_to([P, D])).then_inc(ld_gffn, 16)
            sp.wait_ge(v_full, VN[("xo", 1, 0)] + 1)
            sp.dma_start(gfin, A["norm_final"].rearrange("(a d) -> a d", a=1).broadcast_to([P, D]))\
                .then_inc(ld_gfin, 16)
            for t in range(T):
                sp.wait_ge(out_ready, t + 1)
                sp.dma_start(out[0, t * P:(t + 1) * P, :], YS[t]).then_inc(out_done, 16)
            sp.wait_ge(out_done, 16 * T)

        @block.gpsimd
        def _(pool):
            def link(ins, n):
                ins.then_inc(pool_ch, 1)
                pool.wait_ge(pool_ch, n)

            link(pool.memset(ident[:], 0.0), 1)
            pool.affine_select(out=ident[:], in_=ident[:], compare_op=ALU.not_equal, fill=1.0, base=0,
                               pattern=[[-1, P]], channel_multiplier=1).then_inc(id_ready, 1)
            pool.memset(relb[:], 1.0).then_inc(rel_one, 1)
            pool.memset(eps[:], EPS).then_inc(eps_ready, 1)
            link(pool.memset(FM[:], 0.0), 2)
            pool.affine_select(out=FM[:], in_=FM[:], compare_op=ALU.is_ge, fill=NEG, base=P,
                               pattern=[[-1, SEQ]], channel_multiplier=1).then_inc(fm_ready, 1)
            pool.iota(iota16[:], [[1, PK]], base=0, channel_multiplier=0,
                      allow_small_or_imprecise_dtypes=True).then_inc(io_ready, 1)
            link(pool.memset(sel[0:NH, :], 0.0), 3)
            sv = sel[0:NH, :].rearrange("p (h x) -> p h x", h=NH)
            pool.affine_select(out=sv, in_=sv, compare_op=ALU.not_equal, fill=1.0, base=0,
                               pattern=[[-1, NH], [0, P]], channel_multiplier=1).then_inc(sel_ready, 1)

            def group(par):
                pool.wait_ge(go_dn[par], 1)
                pool.sem_clear(go_dn[par])
                for u in range(U):
                    pool.indirect_dma_start(DN[u], None, down_rows,
                                            bass.IndirectOffsetOnAxis(ap=ixd[:, par, u:u + 1], axis=0))\
                        .then_inc(dn_in[u], 16)
                pool.wait_ge(go_up[par], 1)
                pool.sem_clear(go_up[par])
                for u in range(U):
                    pool.indirect_dma_start(UPB[par * U + u], None, up_rows,
                                            bass.IndirectOffsetOnAxis(ap=ixu[:, par, u:u + 1], axis=0))\
                        .then_inc(up_in[par * U + u], 16)

            with pool.Fori(0, T * GPT // 2) as i:
                group(0)
                group(1)

        @block.scalar
        def _(act):
            act.dma_start(wf[:, :, :], A["w_in"][0].rearrange("(k p) c -> p k c", p=P)[:, :, 6 * BLK:6 * BLK + NH])\
                .then_inc(ld_wf, 16)
            for r, (name, n) in enumerate((("norm_mix", 8), ("g_moba_out", 4), ("g_fox_out", 4),
                                           ("norm_xattn", 8), ("norm_mem", 8))):
                lo = (0, 8, 12, 16, 24)[r]
                act.dma_start(grow[lo:lo + n, :], A[name][0].rearrange("(k p) -> k p", p=P)).then_inc(ld_gain, 16)
            act.dma_start(bf[:, :], A["b_forget"][0].rearrange("(h a) -> h a", a=1)).then_inc(ld_wf, 16)
            for half, name in enumerate(("peer_subkeys_1", "peer_subkeys_2")):
                act.dma_start(sk_nat[:, :, half * HD:(half + 1) * HD], A[name][0].rearrange("h n d -> n h d"))\
                    .then_inc(ld_sk, 16)
            act.wait_ge(rel_one, 1)
            act.dma_start(relb[0:N_BUCKETS, :], A["rel_bias"]).then_inc(ld_rel, 16)
            act.dma_start(onehot, A["bucket_rows"]).then_inc(ld_rel, 16)

            norm_n = [0]

            def root(src, junk, n, width):
                norm_n[0] += 1
                nc.scalar.activation(junk, src, ACT.Square, accum_out=stat[:, n:n + 1]).then_inc(sum_done, 1)
                act.wait_ge(sum_done, norm_n[0])
                nc.scalar.activation(stat[:, n:n + 1], stat[:, n:n + 1], ACT.Sqrt, bias=eps[:, 0:1],
                                     scale=1.0 / width).then_inc(sq_done, 1)

            def job(key):
                act.wait_ge(a_full, AN[key] + 1)
                return ab[AN[key] % 2]

            act.wait_ge(eps_ready, 1)
            for m in range(2):
                act.wait_ge(ld_mem, 16)
                root(MEM[m], V[:, m, :], m, D)
            for t in range(T):
                act.wait_ge(ld_x[t], 16)
                act.wait_ge(sq_done, 2)
                root(X[t], V[:, t, :], 2 + t, D)
            src = job(("bias",))
            act.copy(brow, src[0:NH, 0:FDIST]).then_inc(a_free, 1)
            for b in range(2):
                for i in range(2):
                    src = job(("mK", b, i))
                    act.copy(KM[:, 4 * b + 2 * i:4 * b + 2 * i + 2, :],
                             src[:, :].rearrange("p (c x) -> p c x", c=2)).then_inc(a_free, 1)
            for b in range(2):
                for m in range(2):
                    src = job(("mV", b, m))
                    act.copy(VM[:, m, b * BLK:(b + 1) * BLK], src[:, :]).then_inc(a_free, 1)

            def forget():
                act.wait_ge(fz, 1)
                nc.scalar.activation(small[:, 2, :], small[:, 2, :], ACT.Exp).then_inc(fe, 1)
                act.wait_ge(fe1, 1)
                nc.scalar.activation(small[:, 2, :], small[:, 2, :], ACT.Ln).then_inc(fl, 1)

            for b in range(6):
                src = job(("win", b, 1))
                if b in (2, 5):
                    act.copy(V[:, 1, (b // 3) * BLK:(b // 3 + 1) * BLK], src[:, :]).then_inc(a_free, 1)
                else:
                    dst = (Q if b % 3 == 0 else K)[:, :, (b // 3) * 4 + 2:(b // 3) * 4 + 4, :]
                    act.mul(dst.rearrange("p t c x -> p c t x"),
                            src[:, :].rearrange("p (c t x) -> p c t x", c=2, t=2),
                            HD ** -0.5 if b % 3 == 0 else 1.0).then_inc(a_free, 1)
                if b == 0:
                    forget()

            for t in range(T):
                nk = (t + 1) * P
                for h in range(2 * NH + 1):
                    if h < 2 * NH:
                        n = t * 2 * NH + h
                        act.wait_ge(v_free, VN[("S", t, h)] + 1)
                        if n >= 2:
                            act.wait_ge(a_full, AN[("PT", (n - 2) // 16, (n - 2) % 16)] + 1)
                        nc.scalar.activation(Pr[:, n % 2, 0:nk], Ssb[:, n % 2, 0:nk], ACT.Exp,
                                             bias=nmx[:, n % 2:n % 2 + 1], scale=-1.0,
                                             accum_out=rsum[:, h:h + 1]).then_inc(p_ready, 1)
                    if h >= 1:
                        src = job(("PT", t, h - 1))
                        n = t * 2 * NH + h - 1
                        act.copy(PT[:, n % 2, 0:nk], src[:, 0:nk]).then_inc(a_free, 1)
                for g in range(2):
                    act.wait_ge(o_raw, 2 * t + g + 1)
                    lo = g * BLK
                    root(HTpage[t][:, lo:lo + BLK], QKVB[:, t, lo:lo + BLK], 4 + 2 * t + g, BLK)

            def piece(t, name):
                if name == "norm_x":
                    act.wait_ge(v_free, VN[("wout", t, 1)] + 1)
                    root(X[t], XS[:, :], 8 + 2 * t, D)
                elif name in ("xq0", "xq1"):
                    b = int(name[2])
                    src = job(("xq", t, b))
                    act.mul(XQ[:, 4 * b:4 * b + 4, :], src[:, :].rearrange("p (c x) -> p c x", c=4),
                            XHD ** -0.5).then_inc(a_free, 1)
                elif name[0] == "h":
                    h = int(name[1])
                    n = t * XH_N + h
                    src = job(("xS", t, h))
                    act.wait_ge(xmax, n + 1)
                    nc.scalar.activation(Pr[:, n % 2, :], src[:, 0:M], ACT.Exp, bias=nmx[:, n % 2:n % 2 + 1],
                                         accum_out=xsum[:, n % 2:n % 2 + 1]).then_inc(a_free, 1)
                    src = job(("xPT", t, h))
                    act.copy(PT[:, n % 2, :], src[:, 0:M]).then_inc(a_free, 1)
                elif name == "norm_p":
                    act.wait_ge(v_free, VN[("xo", t, 1)] + 1)
                    root(X[t], XS[:, :], 9 + 2 * t, D)
                elif name in ("wq0", "wq1"):
                    b = int(name[2])
                    src = job(("wq", t, b))
                    act.copy(QR[t][:, 4 * b:4 * b + 4, :], src[:, :].rearrange("p (c x) -> p c x", c=4))\
                        .then_inc(a_free, 1)
                elif name == "sc":
                    for i in range(4):
                        src = job(("sc", t, i))
                        dst = SALL[t].rearrange("p (h s x) -> p h s x", s=2, x=NKEY)
                        act.copy(dst[:, 4 * (i // 2):4 * (i // 2) + 4, i % 2, :],
                                 src[:, :].rearrange("p (h x) -> p h x", h=4)).then_inc(a_free, 1)

            def top_softmax(H):
                act.wait_ge(top_in, H + 1)
                nc.scalar.activation(texp[:], tv[:], ACT.Exp, bias=tneg[:, 0:1], accum_out=tsum[:, 0:1])\
                    .then_inc(top_exp, 1)

            def stage_down(hp2, k):
                nc.scalar.activation(ixd[:, k % 2, :], IDX[:, hp2, k * U:(k + 1) * U], ACT.Copy)\
                    .then_inc(go_dn[k % 2], 1)

            def stage_up(hp2, k):
                nc.scalar.activation(ixu[:, k % 2, :], IDX[:, hp2, k * U:(k + 1) * U], ACT.Copy)\
                    .then_inc(go_up[k % 2], 1)

            def group(H, hp2, k, first=False, last=False):
                g = H * GPH + k
                par = k % 2
                act.wait_ge(dot_done, (g + 1) * U)
                nc.scalar.activation(gel[:, par, :], dots[:, par, :], ACT.Gelu).then_inc(gelu_done, 1)
                if last:
                    return
                if k == GPH - 1:
                    act.wait_ge(idx_ready, H + 2)
                nxt = (1 - hp2, 0) if k == GPH - 1 else (hp2, k + 1)
                stage_down(*nxt)
                if not first:
                    act.wait_ge(up_used, g)
                stage_up(*nxt)

            for name in CHAIN:
                piece(0, name)
            top_softmax(0)
            act.wait_ge(idx_ready, 1)
            stage_down(0, 0)
            stage_up(0, 0)
            for g in range(GPT):
                group(g // GPH, g // GPH % 2, g % GPH, first=g == 0)
                if g in AFTER:
                    piece(1, AFTER[g])
                if g % GPH == 0:
                    top_softmax(g // GPH + 1)
            act.wait_ge(y_out, 1)
            root(YS[0], HTpage[0], 12 + 0, D)

            def head(H, hp2, last=False):
                for k in range(GPH):
                    group(H, hp2, k, last=last and k == GPH - 1)
                    if k == 0 and not last:
                        top_softmax(H + 1)

            with act.Fori(PH, 2 * PH - 2, 2) as H:
                head(H, 0)
                head(H + 1, 1)
            head(2 * PH - 2, 0)
            head(2 * PH - 1, 1, last=True)
            act.wait_ge(y_out, 2)
            root(YS[1], HTpage[1], 12 + 1, D)

        @block.vector
        def _(dve):
            chain = [0]

            def mark(ins):
                ins.then_inc(dve_ch, 1)
                chain[0] += 1
                return chain[0]

            def link(ins):
                dve.wait_ge(dve_ch, mark(ins))

            def job(key):
                dve.wait_ge(v_full, VN[key] + 1)
                return vb[VN[key] % 2]

            def rstd(col):
                link(nc.vector.reciprocal(stat[:, col:col + 1], stat[:, col:col + 1]))

            def spread(c0, n):
                return gcol[:, c0:c0 + n].unsqueeze(2).broadcast_to([P, n, P])

            def gained(key, half, dst, c0):
                src = job(key)
                nc.vector.tensor_tensor(dst[:, 4 * half:4 * half + 4, :],
                                        src[:, :].rearrange("p (c x) -> p c x", c=4),
                                        spread(c0 + 4 * half, 4), ALU.mult).then_inc(v_free, 1)

            src = job(("gains",))
            nc.vector.tensor_copy(gcol[:, :], src[:, 0:32]).then_inc(v_free, 1)
            dve.wait_ge(v_free, 1)
            for i in range(2):
                src = job(("skT", i))
                nc.vector.tensor_copy(skT[:, 4 * i:4 * i + 4, :], src[:, :].rearrange("p (c x) -> p c x", c=4))\
                    .then_inc(v_free, 1)
            for m in range(2):
                dve.wait_ge(sq_done, m + 1)
                rstd(m)
                nc.vector.tensor_scalar(MEM[m], MEM[m], stat[:, m:m + 1], None, ALU.mult).then_inc(xs_done, 1)
            for m in range(2):
                for i in range(2):
                    gained(("memT", m, i), i, MEMT[m], 24)
            for t in range(T):
                dve.wait_ge(sq_done, 3 + t)
                rstd(2 + t)
                nc.vector.tensor_scalar(V[:, t, :], X[t], stat[:, 2 + t:3 + t], None, ALU.mult)\
                    .then_inc(xs_done, 1)
            for t in range(T):
                for i in range(2):
                    gained(("hT", t, i), i, HT[t], 0)

            src = job(("forget",))
            dve.wait_ge(ld_wf, 32)
            nc.vector.tensor_scalar(small[:, 0, :], src[0:NH, 0:SEQ], bf[:, 0:1], None, ALU.add).then_inc(v_free, 1)
            dve.wait_ge(v_free, VN[("forget",)] + 1)
            link(nc.vector.tensor_scalar(small[:, 1, :], small[:, 0, :], 0.0, None, ALU.min))
            nc.vector.scalar_tensor_tensor(out=small[:, 2, :], in0=small[:, 1, :], scalar=2.0, in1=small[:, 0, :],
                                           op0=ALU.mult, op1=ALU.subtract).then_inc(fz, 1)

            def forget_sum():
                dve.wait_ge(fe, 1)
                nc.vector.tensor_scalar(small[:, 2, :], small[:, 2, :], 1.0, None, ALU.add).then_inc(fe1, 1)
                dve.wait_ge(fl, 1)
                link(nc.vector.tensor_tensor(small[:, 3, :], small[:, 2, :], small[:, 1, :], ALU.subtract))
                nc.vector.tensor_tensor_scan(small[:, 0, :], small[:, 3, :], small[:, 3, :], 0.0,
                                             ALU.add, ALU.bypass).then_inc(nc_ready, 1)

            for b in range(6):
                src = job(("win", b, 0))
                if b in (2, 5):
                    nc.vector.tensor_copy(V[:, 0, (b // 3) * BLK:(b // 3 + 1) * BLK], src[:, :]).then_inc(v_free, 1)
                else:
                    dst = (Q if b % 3 == 0 else K)[:, :, (b // 3) * 4:(b // 3) * 4 + 2, :]
                    nc.vector.tensor_scalar(dst.rearrange("p t c x -> p c t x"),
                                            src[:, :].rearrange("p (c t x) -> p c t x", c=2, t=2),
                                            HD ** -0.5 if b % 3 == 0 else 1.0, None, ALU.mult).then_inc(v_free, 1)
                if b == 0:
                    forget_sum()

            dve.wait_ge(ld_bias, 16 * NH)
            dve.wait_ge(fm_ready, 1)
            for t in range(T):
                nk = (t + 1) * P
                lo = SEQ - nk
                for h in range(2 * NH):
                    n = t * 2 * NH + h
                    src = job(("S", t, h))
                    if n >= 2:
                        dve.wait_ge(p_ready, n - 1)
                    add = B[:, h, lo:SEQ] if h < NH else FM[:, lo:SEQ]
                    nc.vector.tensor_tensor_reduce(out=Ssb[:, n % 2, 0:nk], in0=src[:, 0:nk], in1=add,
                                                   scale=-1.0, scalar=3e38, op0=ALU.add, op1=ALU.min,
                                                   accum_out=nmx[:, n % 2:n % 2 + 1]).then_inc(v_free, 1)
                dve.wait_ge(p_ready, (t + 1) * 2 * NH)
                link(nc.vector.reciprocal(rinv[:, :], rsum[:, :]))
                for g in range(2):
                    dve.wait_ge(o_full, 2 * t + g + 1)
                    nc.vector.tensor_tensor(
                        HTpage[t][:, g * BLK:(g + 1) * BLK].rearrange("p (h x) -> p h x", h=NH),
                        y[:, g * BLK:(g + 1) * BLK].rearrange("p (h x) -> p h x", h=NH),
                        rinv[:, g * NH:(g + 1) * NH].unsqueeze(2).broadcast_to([P, NH, HD]),
                        ALU.mult).then_inc(o_raw, 1)
            for t in range(T):
                for g in range(2):
                    dve.wait_ge(sq_done, SQ[("oA", t)] + g)
                    rstd(4 + 2 * t + g)
                    part = HTpage[t][:, g * BLK:(g + 1) * BLK]
                    ins = nc.vector.tensor_scalar(part, part, stat[:, 4 + 2 * t + g:5 + 2 * t + g], None, ALU.mult)
                    if g == 0:
                        link(ins)
                    else:
                        ins.then_inc(xs_done, 1)

            def residual(key, t, b):
                src = job(key)
                part = X[t][:, b * BLK:(b + 1) * BLK]
                nc.vector.tensor_tensor(part, src[:, :], part, ALU.add).then_inc(v_free, 1)

            for t in range(T):
                for i in range(2):
                    gained(("oT", t, i), i, Q[:, t, :, :], 8)
                for b in range(2):
                    residual(("wout", t, b), t, b)

            def piece(t, name):
                if name == "norm_x":
                    dve.wait_ge(sq_done, SQ[("xa", t)])
                    rstd(8 + 2 * t)
                    nc.vector.tensor_scalar(XS[:, :], X[t], stat[:, 8 + 2 * t:9 + 2 * t], None, ALU.mult)\
                        .then_inc(xs_done, 1)
                    for i in range(2):
                        gained(("xT", t, i), i, HT[t], 16)
                elif name[0] == "h":
                    h = int(name[1])
                    n = t * XH_N + h
                    dve.wait_ge(a_full, AN[("xS", t, h)] + 1)
                    nc.vector.tensor_reduce(nmx[:, n % 2:n % 2 + 1], ab[AN[("xS", t, h)] % 2][:, 0:M], AX.X,
                                            ALU.max, negate=True).then_inc(xmax, 1)
                    dve.wait_ge(a_free, AN[("xS", t, h)] + 1)
                    link(nc.vector.reciprocal(xinv[:, n % 2:n % 2 + 1], xsum[:, n % 2:n % 2 + 1]))
                    nc.vector.tensor_scalar(Pr[:, n % 2, :], Pr[:, n % 2, :], xinv[:, n % 2:n % 2 + 1], None,
                                            ALU.mult).then_inc(xp, 1)
                    src = job(("xO", t, h))
                    nc.vector.tensor_copy(XQ[:, 2 * h:2 * h + 2, :],
                                          src[:, 0:2 * P].rearrange("p (c x) -> p c x", c=2)).then_inc(v_free, 1)
                elif name in ("xo0", "xo1"):
                    residual(("xo", t, int(name[2])), t, int(name[2]))
                elif name == "norm_p":
                    dve.wait_ge(sq_done, SQ[("pe", t)])
                    rstd(9 + 2 * t)
                    link(nc.vector.tensor_scalar(XS[:, :], X[t], stat[:, 9 + 2 * t:10 + 2 * t], None, ALU.mult))
                    dve.wait_ge(ld_gffn, 16)
                    nc.vector.tensor_tensor(XS[:, :], XS[:, :], gffn[:, :], ALU.mult).then_inc(xs_done, 1)
                    for i in range(2):
                        src = job(("pT", t, i))
                        nc.vector.tensor_copy(HT[t][:, 4 * i:4 * i + 4, :],
                                              src[:, :].rearrange("p (c x) -> p c x", c=4)).then_inc(v_free, 1)

            def top_experts(scores, H, hp2):
                step = [0]

                def t_mark(ins):
                    ins.then_inc(top_ch, 1)
                    step[0] += 1
                    return step[0]

                def after(k):
                    dve.wait_ge(top_ch, k)

                after_copy = t_mark(nc.vector.tensor_copy(sc[:, :, :].rearrange("p a x -> p (a x)"), scores))
                after(after_copy)
                for rnd in range(2):
                    lo = 8 * rnd
                    m = [t_mark(nc.vector.max(kv[:, s, lo:lo + 8], sc[:, s, :])) for s in range(2)]
                    for s in range(2):
                        after(m[s])
                        last = t_mark(nc.vector.max_index(ku[:, s, lo:lo + 8], kv[:, s, lo:lo + 8], sc[:, s, :]))
                    if rnd == 0:
                        for s in range(2):
                            last = t_mark(nc.vector.match_replace(sc[:, s, :], kv[:, s, 0:8], sc[:, s, :], -3e38))
                    after(last)
                last = t_mark(nc.vector.tensor_copy(kf[:, :, :], ku[:, :, :]))
                cv = cand[:, :].rearrange("p (a b) -> p a b", a=PK)
                last = t_mark(nc.vector.tensor_tensor(cv, kv[:, 0, :].unsqueeze(2).broadcast_to([P, PK, PK]),
                                                      kv[:, 1, :].unsqueeze(1).broadcast_to([P, PK, PK]), ALU.add))
                after(last)
                for rnd in range(2):
                    lo = 8 * rnd
                    after(t_mark(nc.vector.max(tv[:, lo:lo + 8], cand[:, :])))
                    last = t_mark(nc.vector.max_index(pos[:, lo:lo + 8], tv[:, lo:lo + 8], cand[:, :]))
                    if rnd == 0:
                        last = t_mark(nc.vector.match_replace(cand[:, :], tv[:, 0:8], cand[:, :], -3e38))
                    after(last)
                nc.vector.tensor_scalar(tneg[:, 0:1], tv[:, 0:1], -1.0, None, ALU.mult).then_inc(top_in, 1)
                t_mark(nc.vector.tensor_scalar(pab[:, 0, :], pos[:, :], 4, None, ALU.logical_shift_right))
                last = t_mark(nc.vector.tensor_scalar(pab[:, 1, :], pos[:, :], 15, None, ALU.bitwise_and))
                after(last)
                after(t_mark(nc.vector.tensor_copy(pabf[:, :, :], pab[:, :, :])))
                for s in range(2):
                    last = t_mark(nc.vector.tensor_tensor(
                        hot[:, s, :, :], pabf[:, s, :].unsqueeze(2).broadcast_to([P, PK, PK]),
                        iota16[:, :].unsqueeze(1).broadcast_to([P, PK, PK]), ALU.is_equal))
                after(last)
                for s in range(2):
                    last = t_mark(nc.vector.tensor_tensor(
                        hot[:, s, :, :], hot[:, s, :, :],
                        kf[:, s, :].unsqueeze(1).broadcast_to([P, PK, PK]), ALU.mult))
                after(last)
                after(t_mark(nc.vector.tensor_reduce(picked[:, :, :], hot[:, :, :, :], AX.X, ALU.add)))
                dve.wait_ge(top_exp, H + 1)
                after(t_mark(nc.vector.reciprocal(tinv[:, :], tsum[:, :])))
                after(t_mark(nc.vector.tensor_scalar(GATE[:, hp2, :], texp[:, :], tinv[:, 0:1], None, ALU.mult)))
                dve.sem_clear(top_ch)
                nc.vector.scalar_tensor_tensor(out=IDX[:, hp2, :], in0=picked[:, 0, :], scalar=float(NKEY),
                                               in1=picked[:, 1, :], op0=ALU.mult, op1=ALU.add).then_inc(idx_ready, 1)

            def top_static(H):
                t, h = H // PH, H % PH
                dve.wait_ge(a_free, AN[("sc", t, 3)] + 1)
                top_experts(SALL[t][:, h * 2 * NKEY:(h + 1) * 2 * NKEY], H, H % 2)

            def group(H, hp2, k):
                g, par = H * GPH + k, k % 2
                for u in range(U):
                    dve.wait_ge(dn_in[u], (g + 1) * 16)
                    ins = nc.vector.tensor_tensor_reduce(out=DN[u], in0=hp[:, :], in1=DN[u], scale=1.0, scalar=0.0,
                                                         op0=ALU.mult, op1=ALU.add,
                                                         accum_out=dots[:, par, u:u + 1])
                    ins.then_inc(dot_done, 1)
                dve.wait_ge(gelu_done, g + 1)
                ins = nc.vector.tensor_tensor(wgt[:, par, :], gel[:, par, :], GATE[:, hp2, k * U:(k + 1) * U], ALU.mult)
                ins.then_inc(w_done, 1)
                dve.wait_ge(w_done, g + 1)
                if not isinstance(g, int) or g >= 2:
                    dve.wait_ge(up_used, g - 1)
                for u in range(U):
                    ins = nc.vector.tensor_scalar(diag[:, par, u, :], ident[:, :], wgt[:, par, u:u + 1], None, ALU.mult)
                ins.then_inc(diag_done, 1)

            def start_tile(t):
                nc.vector.tensor_copy(hp[:, :], XS[:, :]).then_inc(hp_ready, 1)
                dve.wait_ge(hp_ready, t + 1)

            def rows_out(t):
                dve.wait_ge(up_used, (t + 1) * GPT)
                nc.vector.tensor_copy(YS[t], y[:, :]).then_inc(y_out, 1)

            def finish(t):
                dve.wait_ge(sq_done, SQ[("fin", t)])
                rstd(12 + t)
                dve.wait_ge(ld_gfin, 16)
                nc.vector.scalar_tensor_tensor(out=YS[t], in0=YS[t], scalar=stat[:, 12 + t:13 + t], in1=gfin,
                                               op0=ALU.mult, op1=ALU.mult).then_inc(out_ready, 1)

            for name in CHAIN:
                piece(0, name)
            dve.wait_ge(io_ready, 1)
            top_static(0)
            start_tile(0)
            for g in range(GPT):
                group(g // GPH, g // GPH % 2, g % GPH)
                if g in AFTER:
                    piece(1, AFTER[g])
                if g % GPH == 0:
                    top_static(g // GPH + 1)
            rows_out(0)
            start_tile(1)
            finish(0)
            with dve.Fori(PH, 2 * PH - 2, 2) as H:
                for odd in range(2):
                    for k in range(GPH):
                        group(H + odd, odd, k)
                        if k == 0:
                            top_experts(SALL[1][:, bass.ds((H + (odd + 1 - PH)) * (2 * NKEY), 2 * NKEY)], H + odd + 1,
                                        1 - odd)
            for H in (2 * PH - 2, 2 * PH - 1):
                for k in range(GPH):
                    group(H, H % 2, k)
                    if k == 0 and H < 2 * PH - 1:
                        top_static(H + 1)
            rows_out(1)
            finish(1)

        @block.tensor
        def _(pe):
            def v_job(key):
                n = VN[key]
                if n >= 2:
                    pe.wait_ge(v_free, n - 1)
                return vb[n % 2]

            def a_job(key):
                n = AN[key]
                if n >= 2:
                    pe.wait_ge(a_free, n - 1)
                return ab[n % 2]

            def weights(name, b):
                n = BN[(name, b)]
                pe.wait_ge(w_full[n % W_SLOTS], 16 * (n // W_SLOTS + 1))
                return wblk(name, b)

            def transposes(key, rows, half):
                bank = v_job(key)
                for c in range(4):
                    k = 4 * half + c
                    ins = nc.tensor.transpose(bank[:, c * P:(c + 1) * P], rows[:, k * P:(k + 1) * P], ident[:, :])
                ins.then_inc(v_full, 1)

            def product(bank, lo, n, lhs, rhs, chunks=KC):
                for k in range(chunks):
                    ins = nc.tensor.matmul(bank[:, lo:lo + n], lhs(k), rhs(k), start=(k == 0), stop=(k == chunks - 1))
                return ins

            pe.wait_ge(id_ready, 1)
            pe.wait_ge(ld_gain, 16 * 5)
            bank = v_job(("gains",))
            nc.tensor.transpose(bank[:, 0:32], grow[:, :], ident[0:32, 0:32]).then_inc(v_full, 1)
            pe.wait_ge(ld_sk, 32)
            for i in range(2):
                transposes(("skT", i), sk_nat.rearrange("p h x -> p (h x)"), i)
            for m in range(2):
                pe.wait_ge(xs_done, m + 1)
                for i in range(2):
                    transposes(("memT", m, i), SC[f"mem{m}"], i)
            for t in range(T):
                pe.wait_ge(xs_done, 3 + t)
                for i in range(2):
                    transposes(("hT", t, i), SC[f"x{t}"], i)
            pe.wait_ge(ld_rel, 32)
            bank = a_job(("bias",))
            nc.tensor.matmul(bank[0:NH, 0:FDIST], relb[:, :], onehot, start=True, stop=True).then_inc(a_full, 1)
            pe.wait_ge(v_free, VN[("memT", 1, 1)] + 1)
            for b in range(2):
                w = weights("w_xk", b)
                for i in range(2):
                    bank = a_job(("mK", b, i))
                    for c in range(2):
                        cc = (2 * i + c) * P
                        ins = product(bank, c * M, M, lambda k: w[:, k, cc:cc + P], lambda k: K[:, :, k, :])
                    ins.then_inc(a_full, 1)
            for b in range(2):
                w = weights("w_xv", b)
                for m in range(2):
                    bank = a_job(("mV", b, m))
                    product(bank, 0, BLK, lambda k: MEMT[m][:, k, :], lambda k: w[:, k, :]).then_inc(a_full, 1)

            def h_both(k):
                return XH[:, :, 1, k * P:(k + 1) * P]

            pe.wait_ge(v_free, VN[("hT", 1, 1)] + 1)
            pe.wait_ge(ld_wf, 32)
            bank = v_job(("forget",))
            product(bank[0:NH, :], 0, SEQ, lambda k: wf[:, k, :], h_both).then_inc(v_full, 1)
            for b in range(6):
                w = weights("w_in", b)
                for i, (bank_of, full) in enumerate(((v_job, v_full), (a_job, a_full))):
                    bank = bank_of(("win", b, i))
                    if b in (2, 5):
                        ins = product(bank, 0, BLK, lambda k: HT[i][:, k, :], lambda k: w[:, k, :])
                    else:
                        for c in range(2):
                            cc = (2 * i + c) * P
                            ins = product(bank, c * SEQ, SEQ, lambda k: w[:, k, cc:cc + P], h_both)
                    ins.then_inc(full, 1)

            pe.wait_ge(a_free, AN[("win", 5, 1)] + 1)
            pe.wait_ge(v_free, VN[("win", 5, 0)] + 1)
            pe.wait_ge(nc_ready, 1)
            pe.wait_ge(sel_ready, 1)

            def scores(t, h):
                nk = (t + 1) * P
                bank = v_job(("S", t, h))
                lo, c = (h % 2) * HD, h // 2
                ins = nc.tensor.matmul(bank[:, 0:nk], Q[lo:lo + HD, t, c, :], K[lo:lo + HD, 0:t + 1, c, :],
                                       start=True, stop=h < NH)
                if h >= NH:
                    ins = nc.tensor.matmul(bank[:, 0:nk], sel[0:NH, (h - NH) * P:(h - NH + 1) * P],
                                           small[:, 0, 0:nk], start=False, stop=True)
                ins.then_inc(v_full, 1)

            def probs_t(t, h):
                n = t * 2 * NH + h
                pe.wait_ge(p_ready, n + 1)
                bank = a_job(("PT", t, h))
                for j in range(t + 1):
                    ins = nc.tensor.transpose(bank[:, j * P:(j + 1) * P], Pr[:, n % 2, j * P:(j + 1) * P], ident[:, :])
                ins.then_inc(a_full, 1)

            def values(t, h):
                n = t * 2 * NH + h
                pe.wait_ge(a_free, AN[("PT", t, h)] + 1)
                if t and h % NH == 0:
                    pe.wait_ge(o_raw, 2 * (t - 1) + h // NH + 1)
                for j in range(t + 1):
                    ins = nc.tensor.matmul(y[:, h * HD:(h + 1) * HD], PT[:, n % 2, j * P:(j + 1) * P],
                                           V[:, j, h * HD:(h + 1) * HD], start=(j == 0), stop=(j == t))
                if h % NH == NH - 1:
                    ins.then_inc(o_full, 1)

            for t in range(T):
                scores(t, 0)
                scores(t, 1)
                for h in range(2 * NH):
                    probs_t(t, h)
                    if h + 2 < 2 * NH:
                        scores(t, h + 2)
                    if h >= 1:
                        values(t, h - 1)
                values(t, 2 * NH - 1)
            for t in range(T):
                pe.wait_ge(xs_done, XN[f"o{t}"])
                for i in range(2):
                    transposes(("oT", t, i), HTpage[t], i)
                for b in range(2):
                    w = weights("w_out", b)
                    pe.wait_ge(v_free, VN[("oT", t, 1)] + 1)
                    bank = v_job(("wout", t, b))
                    product(bank, 0, BLK, lambda k: Q[:, t, k, :], lambda k: w[:, k, :]).then_inc(v_full, 1)

            def y_start(t):
                for b in range(2):
                    nc.tensor.matmul(y[:, b * BLK:(b + 1) * BLK], ident[:, :], X[t][:, b * BLK:(b + 1) * BLK],
                                     start=True, stop=False)

            def piece(t, name):
                if name == "norm_x":
                    pe.wait_ge(xs_done, XN[f"xa{t}"])
                    for i in range(2):
                        transposes(("xT", t, i), XS, i)
                elif name in ("xq0", "xq1"):
                    b = int(name[2])
                    w = weights("w_xq", b)
                    pe.wait_ge(v_free, VN[("xT", t, 1)] + 1)
                    bank = a_job(("xq", t, b))
                    for c in range(4):
                        ins = product(bank, c * P, P, lambda k: w[:, k, c * P:(c + 1) * P], lambda k: HT[t][:, k, :])
                    ins.then_inc(a_full, 1)
                elif name[0] == "h":
                    h = int(name[1])
                    n = t * XH_N + h
                    pe.wait_ge(a_free, AN[("xq", t, 1)] + 1)
                    bank = a_job(("xS", t, h))
                    product(bank, 0, M, lambda i: XQ[:, 2 * h + i, :], lambda i: KM[:, 2 * h + i, :], 2)\
                        .then_inc(a_full, 1)
                    pe.wait_ge(xp, n + 1)
                    bank = a_job(("xPT", t, h))
                    for j in range(2):
                        ins = nc.tensor.transpose(bank[:, j * P:(j + 1) * P], Pr[:, n % 2, j * P:(j + 1) * P],
                                                  ident[:, :])
                    ins.then_inc(a_full, 1)
                    pe.wait_ge(a_free, AN[("xPT", t, h)] + 1)
                    bank = v_job(("xO", t, h))
                    for i in range(2):
                        cc = h * XHD + i * P
                        ins = product(bank, i * P, P, lambda j: VM[:, j, cc:cc + P],
                                      lambda j: PT[:, n % 2, j * P:(j + 1) * P], 2)
                    ins.then_inc(v_full, 1)
                elif name in ("xo0", "xo1"):
                    b = int(name[2])
                    w = weights("w_xo", b)
                    pe.wait_ge(v_free, VN[("xO", t, XH_N - 1)] + 1)
                    bank = v_job(("xo", t, b))
                    product(bank, 0, BLK, lambda k: XQ[:, k, :], lambda k: w[:, k, :]).then_inc(v_full, 1)
                elif name == "norm_p":
                    pe.wait_ge(xs_done, XN[f"pe{t}"])
                    for i in range(2):
                        transposes(("pT", t, i), XS, i)
                    if t == 0:
                        y_start(0)
                elif name in ("wq0", "wq1"):
                    b = int(name[2])
                    w = weights("w_peer_query", b)
                    pe.wait_ge(v_free, VN[("pT", t, 1)] + 1)
                    bank = a_job(("wq", t, b))
                    for c in range(4):
                        ins = product(bank, c * P, P, lambda k: w[:, k, c * P:(c + 1) * P], lambda k: HT[t][:, k, :])
                    ins.then_inc(a_full, 1)
                elif name == "sc":
                    pe.wait_ge(a_free, AN[("wq", t, 1)] + 1)
                    for i in range(4):
                        bank = a_job(("sc", t, i))
                        quad, lo = i // 2, (i % 2) * HD
                        for hh in range(4):
                            h = 4 * quad + hh
                            ins = nc.tensor.matmul(bank[:, hh * NKEY:(hh + 1) * NKEY], QR[t][lo:lo + HD, h, :],
                                                   skT[lo:lo + HD, h, :], start=True, stop=True)
                        ins.then_inc(a_full, 1)

            def group(g, g_half, k, last=False):
                par = k % 2
                pe.wait_ge(diag_done, g + 1)
                for u in range(U):
                    pe.wait_ge(up_in[par * U + u], (g_half + 1) * 16)
                    for b in range(2):
                        ins = nc.tensor.matmul(y[:, b * BLK:(b + 1) * BLK], diag[:, par, u, :],
                                               UPB[par * U + u][:, b * BLK:(b + 1) * BLK], start=False,
                                               stop=last and u == U - 1)
                ins.then_inc(up_used, 1)

            for name in CHAIN:
                piece(0, name)
            for g in range(GPT):
                group(g, g // 2, g % GPH, last=g == GPT - 1)
                if g in AFTER:
                    piece(1, AFTER[g])
            pe.wait_ge(y_out, 1)
            y_start(1)
            with pe.Fori(PH, 2 * PH - 1) as H:
                for k in range(GPH):
                    group(H * GPH + k, H * (GPH // 2) + k // 2, k)
            for k in range(GPH):
                g = T * GPT - GPH + k
                group(g, g // 2, k, last=k == GPH - 1)


INPUTS = ["x", "mem", "norm_mix", "w_in", "b_forget", "rel_bias", "g_moba_out", "g_fox_out", "w_out", "norm_xattn",
          "norm_mem", "w_xq", "w_xk", "w_xv", "w_xo", "norm_ffn", "w_peer_query", "peer_subkeys_1",
          "peer_subkeys_2", "peer_expert_down", "peer_expert_up", "norm_final"]


def kernel(**inputs):
    import concourse.bacc as bacc
    from concourse.bass_utils import run_bass_kernel_spmd as run

    nc = bacc.Bacc("TRN2", target_bir_lowering=False, num_devices=1)
    arrays, aps = {}, {}
    for name in INPUTS:
        arrays[f"in_{name}"] = np.ascontiguousarray(inputs[name])
    arrays["in_bucket_rows"] = bucket_rows()
    for key, a in arrays.items():
        aps[key[3:]] = nc.dram_tensor(key, a.shape, mybir.dt.from_np(a.dtype), kind="ExternalInput").ap()
    out = nc.dram_tensor("out", (1, SEQ, D), mybir.dt.float32, kind="ExternalOutput").ap()
    bias_scratch = nc.dram_tensor("bias_scratch", (NH, P, FDIST), mybir.dt.float32).ap()
    hybrid_layer(nc, aps, out, bias_scratch)
    r = run(nc, [arrays], core_ids=[0])
    return r.results[0]["out"]
```

```python
import math
from contextlib import ExitStack

import numpy as np
import concourse.bass as bass
from concourse import mybir

P = 128
D = 1024
SEQ = 256
T = SEQ // P
M = 256
KC = D // P
HD = 64
NH = 8
BLK = 512
XH_N, XHD = 4, 256
PH, PK = 8, 16
NKEY = 128
N_BUCKETS, MAX_DISTANCE = 32, 128
EPS = 1e-6
NEG = -1e30
W_SLOTS = 7
U = 2
DEPTH = 3
GPH = PK // U
GPT = PH * GPH
FDIST = 384


def bucket_rows():
    max_exact = N_BUCKETS // 2
    rows = np.zeros((N_BUCKETS + 1, FDIST), np.float32)
    for m in range(FDIST):
        d = (SEQ - 1) - m
        if d < 0:
            rows[N_BUCKETS, m] = NEG
            continue
        b = d
        if d >= max_exact:
            b = min(max_exact + int(math.log(d / max_exact) / math.log(MAX_DISTANCE / max_exact)
                                    * (N_BUCKETS - max_exact)), N_BUCKETS - 1)
        rows[b, m] = 1.0
    return rows


def hybrid_layer(nc, A, out, bias_scratch):
    f32, i32, u32 = mybir.dt.float32, mybir.dt.int32, mybir.dt.uint32
    ALU, ACT, AX = mybir.AluOpType, mybir.ActivationFunctionType, mybir.AxisListType

    down_rows = A["peer_expert_down"].rearrange("l e d -> (l e) d")
    up_rows = A["peer_expert_up"].rearrange("l e d -> (l e) d")

    blocks = []
    for name, cols in (("w_xk", 2), ("w_xv", 2), ("w_in", 6), ("w_out", 2), ("w_xq", 2), ("w_xo", 2),
                       ("w_peer_query", 2)):
        blocks += [(name, b) for b in range(cols)]
    BN = {key: n for n, key in enumerate(blocks)}

    def heads(t, lo, hi):
        out = []
        for h in range(lo, min(lo + 2, hi)):
            out += [("S", t, h)]
        for h in range(lo, hi):
            out += [("PT", t, h)]
            if h + 2 < hi:
                out += [("S", t, h + 2)]
            if h > lo:
                out += [("O", t, h - 1)]
        return out + [("O", t, hi - 1)]

    def xheads(t):
        out = [("xS", t, 0), ("xS", t, 1)]
        for h in range(XH_N):
            out += [("xnorm", t, h), ("xPT", t, h)]
            if h + 2 < XH_N:
                out += [("xS", t, h + 2)]
            if h > 0:
                out += [("xO", t, h - 1)]
        return out + [("xO", t, XH_N - 1)]

    main = [("gains", 0, 0), ("root_m", 0, 0), ("root_m", 0, 1), ("root_h", 0, 0), ("root_h", 1, 0),
            ("scale_m", 0, 0), ("scale_m", 0, 1), ("memT", 0, 0), ("memT", 0, 1), ("memT", 1, 0), ("memT", 1, 1),
            ("scale_h", 0, 0), ("scale_h", 1, 0), ("mK", 0, 0), ("mK", 0, 1)]
    main += [("hT", t, i) for t in range(T) for i in range(2)]
    main += [("bias", 0, 0), ("mK", 1, 0), ("mK", 1, 1)] + [("mV", b, m) for b in range(2) for m in range(2)]
    main += [("forget", 0, 0), ("skT", 0, 0), ("skT", 0, 1)]
    for b in range(6):
        main += [("winv", b, 0), ("wina", b, 1)]
        if b == 0:
            main += [("fsum", 0, 0)]
    main += heads(0, 0, 2 * NH) + [("o_out", 0, 0), ("o_out", 0, 1), ("o_root", 0, 0), ("o_root", 0, 1)]
    main += [("S", 1, 0), ("S", 1, 1), ("o_scale", 0, 0)] + heads(1, 0, NH)[2:]
    main += [("oT", 0, 0), ("oT", 0, 1), ("wout", 0, 0), ("wout", 0, 1), ("root_x", 0, 0)]
    main += [("S", 1, NH), ("S", 1, NH + 1), ("scale_x", 0, 0)] + heads(1, NH, 2 * NH)[2:]
    main += [("o_out", 1, 0), ("o_out", 1, 1), ("o_root", 1, 0), ("o_root", 1, 1)]
    main += [("xT", 0, 0), ("xT", 0, 1), ("xq", 0, 0), ("xq", 0, 1), ("o_scale", 1, 0)]
    xh = xheads(0)
    main += xh[:2] + [("oT", 1, 0), ("oT", 1, 1)] + xh[2:5] + [("wout", 1, 0)] + xh[5:]
    main += [("xo", 0, 0), ("xo", 0, 1), ("root_p", 0, 0), ("wout", 1, 1), ("scale_p", 0, 0), ("pT", 0, 0),
             ("pT", 0, 1), ("y_start", 0, 0), ("wq", 0, 0), ("wq", 0, 1)] + [("sc", 0, i) for i in range(4)]

    slots = [(1, ("root_x", 1, 0)), (2, ("scale_x", 1, 0)), (3, ("xT", 1, 0)), (3, ("xT", 1, 1)),
             (6, ("xq", 1, 0)), (9, ("xq", 1, 1))]
    for h in range(XH_N):
        slots += [(12 + 4 * h, ("xS", 1, h)), (15 + 4 * h, ("xnorm", 1, h)), (16 + 4 * h, ("xPT", 1, h)),
                  (19 + 4 * h, ("xO", 1, h))]
    slots += [(34, ("xo", 1, 0)), (37, ("xo", 1, 1)), (40, ("root_p", 1, 0)), (41, ("scale_p", 1, 0)),
              (42, ("pT", 1, 0)), (42, ("pT", 1, 1)), (45, ("wq", 1, 0)), (48, ("wq", 1, 1)),
              (51, ("sc", 1, 0)), (51, ("sc", 1, 1)), (54, ("sc", 1, 2)), (54, ("sc", 1, 3))]
    OWN = ("root_x", "scale_x", "xnorm", "root_p", "scale_p")
    LAG = 2

    def after_group(g, products):
        if products:
            own = [(at, i, st) for i, (at, st) in enumerate(slots) if at == g]
            own.sort(key=lambda e: (e[2][0] in ("xPT",), e[1]))
        else:
            own = [(at, i, st) for i, (at, st) in enumerate(slots)
                   if (at if st[0] in OWN else at + LAG) == g]
            own.sort(key=lambda e: (e[2][0] in ("xPT",), e[1]))
        return [st for _, _, st in own]

    TOP_AT = {1: "keys", 2: "sums", 3: "experts"}

    ordered = main + [st for g in range(GPT) for st in after_group(g, True)]
    v_jobs = [st for st in ordered if st[0] in ("gains", "memT", "hT", "forget", "skT", "winv", "S", "oT", "wout",
                                                "xT", "xO", "xo", "pT")]
    a_jobs = [st for st in ordered if st[0] in ("bias", "mK", "mV", "wina", "PT", "xS", "xPT", "xq", "wq", "sc")]
    VN = {key: n for n, key in enumerate(v_jobs)}
    AN = {key: n for n, key in enumerate(a_jobs)}

    ctx = ExitStack()
    with ctx:
        def sb(name, shape, dt=f32):
            return ctx.enter_context(nc.sbuf_tensor(name, shape, dt))

        def pb(name, shape, dt=f32):
            return ctx.enter_context(nc.psum_tensor(name, shape, dt))

        def sem(name):
            return ctx.enter_context(nc.semaphore(name))

        W = sb("weights", [P, W_SLOTS, KC * BLK])
        QKVB = sb("qkvb", [P, 8, D])
        Q = QKVB[:, 0:2, :].rearrange("p t (c x) -> p t c x", c=KC)
        K = QKVB[:, 2:4, :].rearrange("p t (c x) -> p t c x", c=KC)
        V = QKVB[:, 4:6, :]
        B = QKVB[:, 6:8, :].rearrange("p a (h x) -> p (a h) x", h=4)
        XH = sb("x_and_h", [P, T, 2, D])
        X = [XH[:, t, 0, :] for t in range(T)]
        HTpage = [XH[:, t, 1, :] for t in range(T)]
        HT = [h.rearrange("p (c x) -> p c x", c=KC) for h in HTpage]
        KM = sb("mem_k", [P, KC, M])
        VM = sb("mem_v", [P, 2, D])
        XS = sb("scaled", [P, D])
        XQ = XS[:, :].rearrange("p (c x) -> p c x", c=KC)
        gffn = sb("gffn", [P, D])
        ident = sb("ident", [P, P])
        FM = sb("fox_mask", [P, SEQ])
        Ssb = sb("s_sb", [P, 2, SEQ])
        Pr = sb("probs", [P, 2, SEQ])
        PT = sb("probs_t", [P, 2, SEQ])
        skT = sb("subkeys_t", [P, PH, NKEY])
        grow = sb("gain_rows", [32, P])
        gcol = sb("gain_cols", [P, 32])
        wf = sb("w_forget", [P, KC, NH])
        bf = sb("b_forget_col", [NH, 1])
        relb = sb("rel_rows", [N_BUCKETS + 1, NH])
        stat = sb("stat", [P, 16])
        eps = sb("eps", [P, 1])
        nmx = sb("neg_max", [P, 2])
        rsum = sb("row_sum", [P, T, 2 * NH])
        rinv = sb("row_inv", [P, T, 2 * NH])
        xsum = sb("x_sum", [P, 2])
        xinv = sb("x_inv", [P, 2])
        kv = sb("key_vals", [P, 2, PK])
        ku = sb("key_idx", [P, 2, PK], u32)
        kf = sb("key_idx_f", [P, 2, PK])
        tv = sb("top_vals", [P, PK])
        pos = sb("top_pos", [P, PK], u32)
        pab = sb("pos_ab", [P, 2, PK], u32)
        pabf = sb("pos_ab_f", [P, 2, PK])
        hot = sb("one_hot", [P, 2, PK, PK])
        iota16 = sb("iota16", [P, PK])
        picked = sb("picked", [P, 2, PK])
        tneg = sb("top_neg", [P, 1])
        texp = sb("top_exp", [P, PK])
        tsum = sb("top_sum", [P, 1])
        tinv = sb("top_inv", [P, 1])
        IDX = sb("expert_idx", [P, 3, PK])
        GATE = sb("gates", [P, 3, PK])
        ixd = sb("ix_down", [P, DEPTH, U], i32)
        ixu = sb("ix_up", [P, DEPTH, U], i32)
        dots = sb("dots", [P, DEPTH, U])
        gel = sb("gelu", [P, DEPTH, U])
        wgt = sb("wgt", [P, DEPTH, U])
        diag = sb("diag", [P, DEPTH, U, P])
        small = diag[0:NH, :, :, :].rearrange("p a b x -> p a (b x)")
        cand = Ssb[:, 0, :]
        sc = Ssb[:, 1, :].rearrange("p (a x) -> p a x", a=2)

        DN = [QKVB[:, i, :] for i in range(DEPTH * U)]
        free_slot = BN[("w_out", 1)] % W_SLOTS
        UPB = [W[:, free_slot, i * D:(i + 1) * D] for i in range(4)]
        UPB += [QKVB[:, i, :] for i in (6, 7)]

        def wslot(name, b):
            return BN[(name, b)] % W_SLOTS

        def wblk(name, b):
            return W[:, wslot(name, b), :].rearrange("p (k c) -> p k c", k=KC)

        SALL = [XH[:, 0, :, :].rearrange("p a x -> p (a x)"), W[:, wslot("w_xq", 1), 0:2 * D]]
        QR = [W[:, free_slot, 0:D].rearrange("p (h x) -> p h x", h=PH),
              W[:, wslot("w_xq", 0), 0:D].rearrange("p (h x) -> p h x", h=PH)]
        gfin = W[:, wslot("w_xo", 0), 0:D]
        sk_nat = gffn[:, :].rearrange("p (h x) -> p h x", h=PH)
        sel = gffn
        brow = Pr[0:NH, :, :].rearrange("p a x -> p (a x)")[:, 0:FDIST]
        onehot = Ssb[0:N_BUCKETS + 1, :, :].rearrange("p a x -> p (a x)")[:, 0:FDIST]
        YS = X

        vb = [pb(f"v_bank{i}", [P, BLK]) for i in range(2)]
        ab = [pb(f"a_bank{i}", [P, BLK]) for i in range(2)]
        y = pb("y", [P, D])
        hp = pb("h_psum", [P, D])

        v_full, v_free = sem("v_full"), sem("v_free")
        a_full, a_free = sem("a_full"), sem("a_free")
        ld_x = [sem(f"ld_x{t}") for t in range(T)]
        ld_mem = [sem(f"ld_mem{m}") for m in range(2)]
        ld_gain, ld_sk, ld_rel, ld_wf, ld_gffn, ld_gfin = (sem("ld_gain"), sem("ld_sk"), sem("ld_rel"),
                                                           sem("ld_wf"), sem("ld_gffn"), sem("ld_gfin"))
        w_full = [sem(f"w_full{i}") for i in range(W_SLOTS)]
        id_ready, fm_ready, rel_one, sel_ready, io_ready = (sem("id_ready"), sem("fm_ready"), sem("rel_one"),
                                                            sem("sel_ready"), sem("io_ready"))
        pool_ch, eps_ready = sem("pool_ch"), sem("eps_ready")
        sum_done = sem("sum_done")
        sq_done = sem("sq_done")
        xs_done = sem("xs_done")
        brow_out, ld_bias = sem("brow_out"), sem("ld_bias")
        fz, fe, fe1, fl, nc_ready = sem("fz"), sem("fe"), sem("fe1"), sem("fl"), sem("nc_ready")
        p_ready, o_full = sem("p_ready"), sem("o_full")
        o_raw = sem("o_raw")
        xmax, xp = sem("xmax"), sem("xp")
        top_in, top_exp, idx_ready = sem("top_in"), sem("top_e"), sem("idx_ready")
        go_dn = [sem(f"go_dn{i}") for i in range(DEPTH)]
        go_up = [sem(f"go_up{i}") for i in range(DEPTH)]
        dn_in = [sem(f"dn_in{i}") for i in range(DEPTH * U)]
        up_in = [sem(f"up_in{i}") for i in range(DEPTH * U)]
        dot_done, gelu_done, diag_done, up_used = (sem("dot_done"), sem("gelu_done"), sem("diag_done"),
                                                   sem("up_used"))
        dve_ch = sem("dve_ch")
        w_done, hp_ready, top_ch = sem("w_done"), sem("hp_ready"), sem("top_ch")
        y_out, out_ready, out_done = sem("y_out"), sem("out_ready"), sem("out_done")

        roots = [st for st in ordered if st[0] in ("root_m", "root_h", "o_root", "root_x", "root_p")]
        roots += [("root_y", 0, 0), ("root_y", 1, 0)]
        SQ = {key: n + 1 for n, key in enumerate(roots)}
        scales = [st for st in main + [st for _, st in slots]
                  if st[0] in ("scale_m", "scale_h", "o_scale", "scale_x", "scale_p")]
        XN = {key: n + 1 for n, key in enumerate(scales)}
        SN = {key[1:]: n for n, key in enumerate(st for st in main if st[0] == "S")}

        def col(name, t, i):
            return {"root_m": i, "root_h": 2 + t, "o_root": 4 + 2 * t + i, "root_x": 8 + 2 * t,
                    "root_p": 9 + 2 * t, "root_y": 12 + t}[name]

        MEM = [Q[:, m, :, :].rearrange("p c x -> p (c x)") for m in range(2)]
        MEMT = [K[:, m, :, :] for m in range(2)]

        block = ctx.enter_context(nc.Block())

        @block.sync
        def _(sp):
            def used_up(name, b):
                if name == "w_out":
                    return v_full, VN[("wout", 1, b)] + 1
                return a_full, AN[({"w_xk": "mK", "w_xv": "mV", "w_in": "wina"}[name], b, 1)] + 1

            def load_block(n):
                name, b = blocks[n]
                if n >= W_SLOTS:
                    sp.wait_ge(*used_up(*blocks[n - W_SLOTS]))
                src = A[name][0].rearrange("(k p) c -> p k c", p=P)[:, :, b * BLK:(b + 1) * BLK]
                sp.dma_start(W[:, n % W_SLOTS, :].rearrange("p (k c) -> p k c", k=KC), src)\
                    .then_inc(w_full[n % W_SLOTS], 16)

            for m in range(2):
                sp.dma_start(QKVB[:, m, :], A["mem"][0, m * P:(m + 1) * P, :]).then_inc(ld_mem[m], 16)
            for t in range(T):
                sp.dma_start(X[t], A["x"][0, t * P:(t + 1) * P, :]).then_inc(ld_x[t], 16)
            for n in range(W_SLOTS):
                load_block(n)
            sp.wait_ge(a_free, AN[("bias", 0, 0)] + 1)
            sp.dma_start(bias_scratch, brow.unsqueeze(1).broadcast_to([NH, P, FDIST])).then_inc(brow_out, 16)
            load_block(W_SLOTS)
            sp.wait_ge(brow_out, 16)
            for h in range(NH):
                toeplitz = bass.AP(tensor=bias_scratch.tensor, offset=h * P * FDIST + P - 1,
                                   ap=[[FDIST - 1, P], [1, SEQ]])
                sp.dma_start(B[:, h, :], toeplitz).then_inc(ld_bias, 16)
            for n in range(W_SLOTS + 1, len(blocks)):
                if n == len(blocks) - 1:
                    sp.wait_ge(v_full, VN[("S", 1, 2 * NH - 1)] + 1)
                    sp.dma_start(gffn[:, :], A["norm_ffn"][0:1, :].broadcast_to([P, D])).then_inc(ld_gffn, 16)
                load_block(n)
            sp.wait_ge(v_full, VN[("xo", 1, 0)] + 1)
            sp.dma_start(gfin, A["norm_final"].rearrange("(a d) -> a d", a=1).broadcast_to([P, D]))\
                .then_inc(ld_gfin, 16)
            for t in range(T):
                sp.wait_ge(out_ready, t + 1)
                sp.dma_start(out[0, t * P:(t + 1) * P, :], YS[t]).then_inc(out_done, 16)
            sp.wait_ge(out_done, 16 * T)

        @block.gpsimd
        def _(pool):
            def link(ins, n):
                ins.then_inc(pool_ch, 1)
                pool.wait_ge(pool_ch, n)

            link(pool.memset(ident[:], 0.0), 1)
            pool.affine_select(out=ident[:], in_=ident[:], compare_op=ALU.not_equal, fill=1.0, base=0,
                               pattern=[[-1, P]], channel_multiplier=1).then_inc(id_ready, 1)
            pool.memset(relb[:], 1.0).then_inc(rel_one, 1)
            pool.memset(eps[:], EPS).then_inc(eps_ready, 1)
            link(pool.memset(FM[:], 0.0), 2)
            pool.affine_select(out=FM[:], in_=FM[:], compare_op=ALU.is_ge, fill=NEG, base=P,
                               pattern=[[-1, SEQ]], channel_multiplier=1).then_inc(fm_ready, 1)
            pool.iota(iota16[:], [[1, PK]], base=0, channel_multiplier=0,
                      allow_small_or_imprecise_dtypes=True).then_inc(io_ready, 1)
            pool.wait_ge(v_free, VN[("skT", 0, 1)] + 1)
            link(pool.memset(sel[0:NH, :], 0.0), 3)
            sv = sel[0:NH, :].rearrange("p (h x) -> p h x", h=NH)
            pool.affine_select(out=sv, in_=sv, compare_op=ALU.not_equal, fill=1.0, base=0,
                               pattern=[[-1, NH], [0, P]], channel_multiplier=1).then_inc(sel_ready, 1)

            def group(par):
                pool.wait_ge(go_dn[par], 1)
                pool.sem_clear(go_dn[par])
                for u in range(U):
                    pool.indirect_dma_start(DN[par * U + u], None, down_rows,
                                            bass.IndirectOffsetOnAxis(ap=ixd[:, par, u:u + 1], axis=0))\
                        .then_inc(dn_in[par * U + u], 16)
                pool.wait_ge(go_up[par], 1)
                pool.sem_clear(go_up[par])
                for u in range(U):
                    pool.indirect_dma_start(UPB[par * U + u], None, up_rows,
                                            bass.IndirectOffsetOnAxis(ap=ixu[:, par, u:u + 1], axis=0))\
                        .then_inc(up_in[par * U + u], 16)

            with pool.Fori(0, T * GPT // DEPTH) as i:
                for par in range(DEPTH):
                    group(par)
            for par in range(T * GPT % DEPTH):
                group(par)

        LOOP_LO, LOOP_HI = PH // 3, PH // 3 + (PH - 2) // 3
        assert 3 * LOOP_LO + 2 == PH and 3 * LOOP_HI + 2 == 2 * PH - 2

        def loop_group(m, j, k):
            rest = (2 + j) * GPH + k
            return m * (3 * GPH) + rest, rest % DEPTH, m * GPH + rest // DEPTH

        def flat_group(H, k):
            g = H * GPH + k
            return g, g % DEPTH, g // DEPTH

        @block.scalar
        def _(act):
            for r, (name, n) in enumerate((("norm_mix", 8), ("g_moba_out", 4), ("g_fox_out", 4),
                                           ("norm_xattn", 8), ("norm_mem", 8))):
                lo = (0, 8, 12, 16, 24)[r]
                act.dma_start(grow[lo:lo + n, :], A[name][0].rearrange("(k p) -> k p", p=P)).then_inc(ld_gain, 16)
            act.wait_ge(rel_one, 1)
            act.dma_start(relb[0:N_BUCKETS, :], A["rel_bias"]).then_inc(ld_rel, 16)
            act.dma_start(onehot, A["bucket_rows"]).then_inc(ld_rel, 16)
            for half, name in enumerate(("peer_subkeys_1", "peer_subkeys_2")):
                act.dma_start(sk_nat[:, :, half * HD:(half + 1) * HD], A[name][0].rearrange("h n d -> n h d"))\
                    .then_inc(ld_sk, 16)
            act.dma_start(bf[:, :], A["b_forget"][0].rearrange("(h a) -> h a", a=1)).then_inc(ld_wf, 16)
            act.dma_start(wf[:, :, :], A["w_in"][0].rearrange("(k p) c -> p k c", p=P)[:, :, 6 * BLK:6 * BLK + NH])\
                .then_inc(ld_wf, 16)

            norm_n = [0]

            def root(key, src, junk, width):
                norm_n[0] += 1
                n = col(*key)
                nc.scalar.activation(junk, src, ACT.Square, accum_out=stat[:, n:n + 1]).then_inc(sum_done, 1)
                act.wait_ge(sum_done, norm_n[0])
                nc.scalar.activation(stat[:, n:n + 1], stat[:, n:n + 1], ACT.Sqrt, bias=eps[:, 0:1],
                                     scale=1.0 / width).then_inc(sq_done, 1)

            def job(key):
                act.wait_ge(a_full, AN[key] + 1)
                return ab[AN[key] % 2]

            def step(name, t, i):
                key = (name, t, i)
                if name == "root_m":
                    act.wait_ge(ld_mem[i], 16)
                    root(key, MEM[i], V[:, i, :], D)
                elif name == "root_h":
                    act.wait_ge(ld_x[t], 16)
                    act.wait_ge(sq_done, 2)
                    root(key, X[t], V[:, t, :], D)
                elif name == "bias":
                    src = job(key)
                    act.copy(brow, src[0:NH, 0:FDIST]).then_inc(a_free, 1)
                elif name == "mK":
                    src = job(key)
                    act.copy(KM[:, 4 * t + 2 * i:4 * t + 2 * i + 2, :],
                             src[:, :].rearrange("p (c x) -> p c x", c=2)).then_inc(a_free, 1)
                elif name == "mV":
                    src = job(key)
                    act.copy(VM[:, i, t * BLK:(t + 1) * BLK], src[:, :]).then_inc(a_free, 1)
                elif name == "fsum":
                    act.wait_ge(fz, 1)
                    nc.scalar.activation(small[:, 2, :], small[:, 2, :], ACT.Exp).then_inc(fe, 1)
                    act.wait_ge(fe1, 1)
                    nc.scalar.activation(small[:, 2, :], small[:, 2, :], ACT.Ln).then_inc(fl, 1)
                elif name == "wina":
                    src, b = job(key), t
                    if b in (2, 5):
                        act.copy(V[:, 1, (b // 3) * BLK:(b // 3 + 1) * BLK], src[:, :]).then_inc(a_free, 1)
                    else:
                        dst = (Q if b % 3 == 0 else K)[:, :, (b // 3) * 4 + 2:(b // 3) * 4 + 4, :]
                        act.mul(dst.rearrange("p t c x -> p c t x"),
                                src[:, :].rearrange("p (c t x) -> p c t x", c=2, t=2),
                                HD ** -0.5 if b % 3 == 0 else 1.0).then_inc(a_free, 1)
                elif name == "S":
                    n, nk = SN[(t, i)], (t + 1) * P
                    act.wait_ge(v_free, VN[key] + 1)
                    if n >= 2:
                        prev = [k for k, v in SN.items() if v == n - 2][0]
                        act.wait_ge(a_full, AN[("PT",) + prev] + 1)
                    nc.scalar.activation(Pr[:, n % 2, 0:nk], Ssb[:, n % 2, 0:nk], ACT.Exp,
                                         bias=nmx[:, n % 2:n % 2 + 1], scale=-1.0,
                                         accum_out=rsum[:, t, i:i + 1]).then_inc(p_ready, 1)
                elif name == "PT":
                    src, n, nk = job(key), SN[(t, i)], (t + 1) * P
                    act.copy(PT[:, n % 2, 0:nk], src[:, 0:nk]).then_inc(a_free, 1)
                elif name == "o_root":
                    act.wait_ge(o_raw, 2 * t + i + 1)
                    root(key, HTpage[t][:, i * BLK:(i + 1) * BLK], QKVB[:, t, i * BLK:(i + 1) * BLK], BLK)
                elif name == "root_x":
                    act.wait_ge(v_free, VN[("wout", t, 1)] + 1)
                    root(key, X[t], XS[:, :], D)
                elif name == "xq":
                    src = job(key)
                    act.mul(XQ[:, 4 * i:4 * i + 4, :], src[:, :].rearrange("p (c x) -> p c x", c=4),
                            XHD ** -0.5).then_inc(a_free, 1)
                elif name == "xS":
                    n = t * XH_N + i
                    src = job(key)
                    act.wait_ge(xmax, n + 1)
                    nc.scalar.activation(Pr[:, n % 2, :], src[:, 0:M], ACT.Exp, bias=nmx[:, n % 2:n % 2 + 1],
                                         accum_out=xsum[:, n % 2:n % 2 + 1]).then_inc(a_free, 1)
                elif name == "xPT":
                    src = job(key)
                    act.copy(PT[:, i % 2, :], src[:, 0:M]).then_inc(a_free, 1)
                elif name == "root_p":
                    act.wait_ge(v_free, VN[("xo", t, 1)] + 1)
                    root(key, X[t], XS[:, :], D)
                elif name == "wq":
                    src = job(key)
                    act.copy(QR[t][:, 4 * i:4 * i + 4, :], src[:, :].rearrange("p (c x) -> p c x", c=4))\
                        .then_inc(a_free, 1)
                elif name == "sc":
                    src = job(key)
                    dst = SALL[t].rearrange("p (h s x) -> p h s x", s=2, x=NKEY)
                    act.copy(dst[:, 4 * (i // 2):4 * (i // 2) + 4, i % 2, :],
                             src[:, :].rearrange("p (h x) -> p h x", h=4)).then_inc(a_free, 1)

            def top_softmax(H):
                act.wait_ge(top_in, H + 1)
                nc.scalar.activation(texp[:], tv[:], ACT.Exp, bias=tneg[:, 0:1], accum_out=tsum[:, 0:1])\
                    .then_inc(top_exp, 1)

            def stage_down(rest):
                par, H3, k = rest % DEPTH, rest // GPH % 3, rest % GPH
                nc.scalar.activation(ixd[:, par, :], IDX[:, H3, k * U:(k + 1) * U], ACT.Copy)\
                    .then_inc(go_dn[par], 1)

            def stage_up(rest):
                par, H3, k = rest % DEPTH, rest // GPH % 3, rest % GPH
                nc.scalar.activation(ixu[:, par, :], IDX[:, H3, k * U:(k + 1) * U], ACT.Copy)\
                    .then_inc(go_up[par], 1)

            def group(H, g, rest, left=GPT):
                par, k = rest % DEPTH, rest % GPH
                act.wait_ge(dot_done, (g + 1) * U)
                nc.scalar.activation(gel[:, par, :], dots[:, par, :], ACT.Gelu).then_inc(gelu_done, 1)
                if left >= 3:
                    if k == GPH - 3:
                        act.wait_ge(idx_ready, H + 2)
                    stage_down(rest + 3)
                if left >= 2:
                    if not isinstance(g, int) or g >= 1:
                        act.wait_ge(up_used, g)
                    stage_up(rest + 2)

            act.wait_ge(eps_ready, 1)
            for st in main:
                step(*st)
            top_softmax(0)
            act.wait_ge(idx_ready, 1)
            for g in range(3):
                stage_down(g)
                if g < 2:
                    stage_up(g)
            for g in range(GPT):
                group(g // GPH, g, g)
                for st in after_group(g, False):
                    step(*st)
                if TOP_AT.get(g % GPH) == "sums":
                    top_softmax(g // GPH + 1)
            act.wait_ge(y_out, 1)
            root(("root_y", 0, 0), YS[0], HTpage[0], D)
            with act.Fori(LOOP_LO, LOOP_HI) as m:
                for j in range(3):
                    for k in range(GPH):
                        group(m * 3 + (2 + j), loop_group(m, j, k)[0], (2 + j) * GPH + k)
                        if TOP_AT.get(k) == "sums":
                            top_softmax(m * 3 + (3 + j))
            for H in (2 * PH - 2, 2 * PH - 1):
                for k in range(GPH):
                    g = H * GPH + k
                    group(H, g, g, left=T * GPT - 1 - g)
                    if TOP_AT.get(k) == "sums" and H < 2 * PH - 1:
                        top_softmax(H + 1)
            act.wait_ge(y_out, 2)
            root(("root_y", 1, 0), YS[1], HTpage[1], D)

        @block.vector
        def _(dve):
            chain = [0]

            def link(ins):
                ins.then_inc(dve_ch, 1)
                chain[0] += 1
                dve.wait_ge(dve_ch, chain[0])

            def job(key):
                dve.wait_ge(v_full, VN[key] + 1)
                return vb[VN[key] % 2]

            def rstd(key):
                dve.wait_ge(sq_done, SQ[key])
                c = col(*key)
                link(nc.vector.reciprocal(stat[:, c:c + 1], stat[:, c:c + 1]))
                return stat[:, c:c + 1]

            def gained(key, half, dst, c0):
                src = job(key)
                gain = gcol[:, c0 + 4 * half:c0 + 4 * half + 4].unsqueeze(2).broadcast_to([P, 4, P])
                nc.vector.tensor_tensor(dst[:, 4 * half:4 * half + 4, :],
                                        src[:, :].rearrange("p (c x) -> p c x", c=4),
                                        gain, ALU.mult).then_inc(v_free, 1)

            def step(name, t, i):
                key = (name, t, i)
                if name == "gains":
                    src = job(key)
                    nc.vector.tensor_copy(gcol[:, :], src[:, 0:32]).then_inc(v_free, 1)
                    dve.wait_ge(v_free, VN[key] + 1)
                elif name == "scale_m":
                    r = rstd(("root_m", 0, i))
                    nc.vector.tensor_scalar(MEM[i], MEM[i], r, None, ALU.mult).then_inc(xs_done, 1)
                elif name == "scale_h":
                    r = rstd(("root_h", t, 0))
                    nc.vector.tensor_scalar(V[:, t, :], X[t], r, None, ALU.mult).then_inc(xs_done, 1)
                elif name == "memT":
                    gained(key, i, MEMT[t], 24)
                elif name == "hT":
                    gained(key, i, HT[t], 0)
                elif name == "skT":
                    src = job(key)
                    nc.vector.tensor_copy(skT[:, 4 * i:4 * i + 4, :], src[:, :].rearrange("p (c x) -> p c x", c=4))\
                        .then_inc(v_free, 1)
                elif name == "forget":
                    src = job(key)
                    dve.wait_ge(ld_wf, 32)
                    nc.vector.tensor_scalar(small[:, 0, :], src[0:NH, 0:SEQ], bf[:, 0:1], None, ALU.add)\
                        .then_inc(v_free, 1)
                    dve.wait_ge(v_free, VN[key] + 1)
                    link(nc.vector.tensor_scalar(small[:, 1, :], small[:, 0, :], 0.0, None, ALU.min))
                    nc.vector.scalar_tensor_tensor(out=small[:, 2, :], in0=small[:, 1, :], scalar=2.0,
                                                   in1=small[:, 0, :], op0=ALU.mult, op1=ALU.subtract)\
                        .then_inc(fz, 1)
                elif name == "fsum":
                    dve.wait_ge(fe, 1)
                    nc.vector.tensor_scalar(small[:, 2, :], small[:, 2, :], 1.0, None, ALU.add).then_inc(fe1, 1)
                    dve.wait_ge(fl, 1)
                    link(nc.vector.tensor_tensor(small[:, 0, :], small[:, 2, :], small[:, 1, :], ALU.subtract))
                    nc.vector.tensor_tensor_scan(small[:, 1, :], small[:, 0, :], small[:, 0, :], 0.0,
                                                 ALU.add, ALU.bypass).then_inc(nc_ready, 1)
                elif name == "winv":
                    src, b = job(key), t
                    if b in (2, 5):
                        nc.vector.tensor_copy(V[:, 0, (b // 3) * BLK:(b // 3 + 1) * BLK], src[:, :])\
                            .then_inc(v_free, 1)
                    else:
                        dst = (Q if b % 3 == 0 else K)[:, :, (b // 3) * 4:(b // 3) * 4 + 2, :]
                        nc.vector.tensor_scalar(dst.rearrange("p t c x -> p c t x"),
                                                src[:, :].rearrange("p (c t x) -> p c t x", c=2, t=2),
                                                HD ** -0.5 if b % 3 == 0 else 1.0, None, ALU.mult)\
                            .then_inc(v_free, 1)
                elif name == "S":
                    n, nk = SN[(t, i)], (t + 1) * P
                    src = job(key)
                    if n == 0:
                        dve.wait_ge(ld_bias, 16 * NH)
                        dve.wait_ge(fm_ready, 1)
                    if n >= 2:
                        dve.wait_ge(p_ready, n - 1)
                    add = B[:, i, SEQ - nk:SEQ] if i < NH else FM[:, SEQ - nk:SEQ]
                    nc.vector.tensor_tensor_reduce(out=Ssb[:, n % 2, 0:nk], in0=src[:, 0:nk], in1=add,
                                                   scale=-1.0, scalar=3e38, op0=ALU.add, op1=ALU.min,
                                                   accum_out=nmx[:, n % 2:n % 2 + 1]).then_inc(v_free, 1)
                elif name == "o_out":
                    if i == 0:
                        dve.wait_ge(p_ready, SN[(t, 2 * NH - 1)] + 1)
                        link(nc.vector.reciprocal(rinv[:, t, :], rsum[:, t, :]))
                    dve.wait_ge(o_full, 2 * t + i + 1)
                    nc.vector.tensor_tensor(
                        HTpage[t][:, i * BLK:(i + 1) * BLK].rearrange("p (h x) -> p h x", h=NH),
                        y[:, i * BLK:(i + 1) * BLK].rearrange("p (h x) -> p h x", h=NH),
                        rinv[:, t, i * NH:(i + 1) * NH].unsqueeze(2).broadcast_to([P, NH, HD]),
                        ALU.mult).then_inc(o_raw, 1)
                elif name == "o_scale":
                    for g in range(2):
                        r = rstd(("o_root", t, g))
                        part = HTpage[t][:, g * BLK:(g + 1) * BLK]
                        ins = nc.vector.tensor_scalar(part, part, r, None, ALU.mult)
                        if g == 0:
                            link(ins)
                        else:
                            ins.then_inc(xs_done, 1)
                elif name == "oT":
                    gained(key, i, Q[:, t, :, :], 8)
                elif name in ("wout", "xo"):
                    src = job(key)
                    part = X[t][:, i * BLK:(i + 1) * BLK]
                    nc.vector.tensor_tensor(part, src[:, :], part, ALU.add).then_inc(v_free, 1)
                elif name == "scale_x":
                    r = rstd(("root_x", t, 0))
                    nc.vector.tensor_scalar(XS[:, :], X[t], r, None, ALU.mult).then_inc(xs_done, 1)
                elif name == "xT":
                    gained(key, i, HT[t], 16)
                elif name == "xS":
                    n = t * XH_N + i
                    dve.wait_ge(a_full, AN[key] + 1)
                    nc.vector.tensor_reduce(nmx[:, n % 2:n % 2 + 1], ab[AN[key] % 2][:, 0:M], AX.X,
                                            ALU.max, negate=True).then_inc(xmax, 1)
                elif name == "xnorm":
                    n = t * XH_N + i
                    dve.wait_ge(a_free, AN[("xS", t, i)] + 1)
                    link(nc.vector.reciprocal(xinv[:, n % 2:n % 2 + 1], xsum[:, n % 2:n % 2 + 1]))
                    nc.vector.tensor_scalar(Pr[:, n % 2, :], Pr[:, n % 2, :], xinv[:, n % 2:n % 2 + 1], None,
                                            ALU.mult).then_inc(xp, 1)
                elif name == "xO":
                    src = job(key)
                    nc.vector.tensor_copy(XQ[:, 2 * i:2 * i + 2, :],
                                          src[:, 0:2 * P].rearrange("p (c x) -> p c x", c=2)).then_inc(v_free, 1)
                elif name == "scale_p":
                    r = rstd(("root_p", t, 0))
                    link(nc.vector.tensor_scalar(XS[:, :], X[t], r, None, ALU.mult))
                    dve.wait_ge(ld_gffn, 16)
                    nc.vector.tensor_tensor(XS[:, :], XS[:, :], gffn[:, :], ALU.mult).then_inc(xs_done, 1)
                elif name == "pT":
                    src = job(key)
                    nc.vector.tensor_copy(HT[t][:, 4 * i:4 * i + 4, :],
                                          src[:, :].rearrange("p (c x) -> p c x", c=4)).then_inc(v_free, 1)

            top_n = [0]

            def t_mark(ins):
                ins.then_inc(top_ch, 1)
                top_n[0] += 1
                return top_n[0]

            def after(k):
                dve.wait_ge(top_ch, k)

            def top_keys(scores):
                top_n[0] = 0
                after(t_mark(nc.vector.tensor_copy(sc[:, :, :].rearrange("p a x -> p (a x)"), scores)))
                for rnd in range(2):
                    lo = 8 * rnd
                    m = [t_mark(nc.vector.max(kv[:, s, lo:lo + 8], sc[:, s, :])) for s in range(2)]
                    for s in range(2):
                        after(m[s])
                        last = t_mark(nc.vector.max_index(ku[:, s, lo:lo + 8], kv[:, s, lo:lo + 8], sc[:, s, :]))
                    if rnd == 0:
                        for s in range(2):
                            last = t_mark(nc.vector.match_replace(sc[:, s, :], kv[:, s, 0:8], sc[:, s, :], -3e38))
                    after(last)
                t_mark(nc.vector.tensor_copy(kf[:, :, :], ku[:, :, :]))
                cv = cand[:, :].rearrange("p (a b) -> p a b", a=PK)
                after(t_mark(nc.vector.tensor_tensor(cv, kv[:, 0, :].unsqueeze(2).broadcast_to([P, PK, PK]),
                                                     kv[:, 1, :].unsqueeze(1).broadcast_to([P, PK, PK]), ALU.add)))

            def top_sums():
                for rnd in range(2):
                    lo = 8 * rnd
                    after(t_mark(nc.vector.max(tv[:, lo:lo + 8], cand[:, :])))
                    last = t_mark(nc.vector.max_index(pos[:, lo:lo + 8], tv[:, lo:lo + 8], cand[:, :]))
                    if rnd == 0:
                        last = t_mark(nc.vector.match_replace(cand[:, :], tv[:, 0:8], cand[:, :], -3e38))
                    after(last)
                nc.vector.tensor_scalar(tneg[:, 0:1], tv[:, 0:1], -1.0, None, ALU.mult).then_inc(top_in, 1)

            def top_experts(H, H3):
                t_mark(nc.vector.tensor_scalar(pab[:, 0, :], pos[:, :], 4, None, ALU.logical_shift_right))
                after(t_mark(nc.vector.tensor_scalar(pab[:, 1, :], pos[:, :], 15, None, ALU.bitwise_and)))
                after(t_mark(nc.vector.tensor_copy(pabf[:, :, :], pab[:, :, :])))
                for s in range(2):
                    last = t_mark(nc.vector.tensor_tensor(
                        hot[:, s, :, :], pabf[:, s, :].unsqueeze(2).broadcast_to([P, PK, PK]),
                        iota16[:, :].unsqueeze(1).broadcast_to([P, PK, PK]), ALU.is_equal))
                after(last)
                for s in range(2):
                    last = t_mark(nc.vector.tensor_tensor(
                        hot[:, s, :, :], hot[:, s, :, :],
                        kf[:, s, :].unsqueeze(1).broadcast_to([P, PK, PK]), ALU.mult))
                after(last)
                after(t_mark(nc.vector.tensor_reduce(picked[:, :, :], hot[:, :, :, :], AX.X, ALU.add)))
                dve.wait_ge(top_exp, H + 1)
                after(t_mark(nc.vector.reciprocal(tinv[:, :], tsum[:, :])))
                after(t_mark(nc.vector.tensor_scalar(GATE[:, H3, :], texp[:, :], tinv[:, 0:1], None, ALU.mult)))
                dve.sem_clear(top_ch)
                nc.vector.scalar_tensor_tensor(out=IDX[:, H3, :], in0=picked[:, 0, :], scalar=float(NKEY),
                                               in1=picked[:, 1, :], op0=ALU.mult, op1=ALU.add).then_inc(idx_ready, 1)

            def top_part(part, H, H3, scores):
                if part == "keys":
                    top_keys(scores)
                elif part == "sums":
                    top_sums()
                elif part == "experts":
                    top_experts(H, H3)

            def static_scores(H):
                return SALL[H // PH][:, (H % PH) * 2 * NKEY:(H % PH + 1) * 2 * NKEY]

            def group(H3, k, g, par, before):
                for u in range(U):
                    dve.wait_ge(dn_in[par * U + u], (before + 1) * 16)
                    ins = nc.vector.tensor_tensor_reduce(out=DN[par * U + u], in0=hp[:, :], in1=DN[par * U + u],
                                                         scale=1.0, scalar=0.0, op0=ALU.mult, op1=ALU.add,
                                                         accum_out=dots[:, par, u:u + 1])
                    ins.then_inc(dot_done, 1)
                dve.wait_ge(gelu_done, g + 1)
                nc.vector.tensor_tensor(wgt[:, par, :], gel[:, par, :], GATE[:, H3, k * U:(k + 1) * U],
                                        ALU.mult).then_inc(w_done, 1)
                dve.wait_ge(w_done, g + 1)
                if not isinstance(g, int) or g >= 3:
                    dve.wait_ge(up_used, g - 2)
                for u in range(U):
                    ins = nc.vector.tensor_scalar(diag[:, par, u, :], ident[:, :], wgt[:, par, u:u + 1], None, ALU.mult)
                ins.then_inc(diag_done, 1)

            def start_tile(t):
                nc.vector.tensor_copy(hp[:, :], XS[:, :]).then_inc(hp_ready, 1)
                dve.wait_ge(hp_ready, t + 1)

            def rows_out(t):
                dve.wait_ge(up_used, (t + 1) * GPT)
                nc.vector.tensor_copy(YS[t], y[:, :]).then_inc(y_out, 1)

            def finish(t):
                r = rstd(("root_y", t, 0))
                dve.wait_ge(ld_gfin, 16)
                nc.vector.scalar_tensor_tensor(out=YS[t], in0=YS[t], scalar=r, in1=gfin,
                                               op0=ALU.mult, op1=ALU.mult).then_inc(out_ready, 1)

            for st in main:
                step(*st)
            dve.wait_ge(io_ready, 1)
            dve.wait_ge(a_free, AN[("sc", 0, 3)] + 1)
            for part in TOP_AT.values():
                top_part(part, 0, 0, static_scores(0))
            start_tile(0)
            for g in range(GPT):
                H = g // GPH
                group(H % 3, g % GPH, *flat_group(H, g % GPH))
                for st in after_group(g, False):
                    step(*st)
                if g == GPT - GPH:
                    dve.wait_ge(a_free, AN[("sc", 1, 3)] + 1)
                top_part(TOP_AT.get(g % GPH), H + 1, (H + 1) % 3, static_scores(H + 1))
            start_tile(1)
            rows_out(0)
            finish(0)
            with dve.Fori(LOOP_LO, LOOP_HI) as m:
                for j in range(3):
                    for k in range(GPH):
                        group((2 + j) % 3, k, *loop_group(m, j, k))
                        top_part(TOP_AT.get(k), m * 3 + (3 + j), (3 + j) % 3,
                                 SALL[1][:, bass.ds((m * 3 + (3 + j - PH)) * (2 * NKEY), 2 * NKEY)])
            for H in (2 * PH - 2, 2 * PH - 1):
                for k in range(GPH):
                    group(H % 3, k, *flat_group(H, k))
                    if H < 2 * PH - 1:
                        top_part(TOP_AT.get(k), H + 1, (H + 1) % 3, static_scores(H + 1))
            rows_out(1)
            finish(1)

        @block.tensor
        def _(pe):
            def v_job(key):
                n = VN[key]
                if n >= 2:
                    pe.wait_ge(v_free, n - 1)
                return vb[n % 2]

            def a_job(key):
                n = AN[key]
                if n >= 2:
                    pe.wait_ge(a_free, n - 1)
                return ab[n % 2]

            def weights(name, b):
                n = BN[(name, b)]
                pe.wait_ge(w_full[n % W_SLOTS], 16 * (n // W_SLOTS + 1))
                return wblk(name, b)

            def transposes(key, rows, half):
                bank = v_job(key)
                for c in range(4):
                    k = 4 * half + c
                    ins = nc.tensor.transpose(bank[:, c * P:(c + 1) * P], rows[:, k * P:(k + 1) * P], ident[:, :])
                ins.then_inc(v_full, 1)

            def product(bank, lo, n, lhs, rhs, chunks=KC):
                for k in range(chunks):
                    ins = nc.tensor.matmul(bank[:, lo:lo + n], lhs(k), rhs(k), start=(k == 0), stop=(k == chunks - 1))
                return ins

            def h_both(k):
                return XH[:, :, 1, k * P:(k + 1) * P]

            def step(name, t, i):
                key = (name, t, i)
                if name == "gains":
                    pe.wait_ge(id_ready, 1)
                    pe.wait_ge(ld_gain, 16 * 5)
                    bank = v_job(key)
                    nc.tensor.transpose(bank[:, 0:32], grow[:, :], ident[0:32, 0:32]).then_inc(v_full, 1)
                elif name == "memT":
                    pe.wait_ge(xs_done, XN[("scale_m", 0, t)])
                    transposes(key, MEM[t], i)
                elif name == "hT":
                    pe.wait_ge(xs_done, XN[("scale_h", t, 0)])
                    transposes(key, V[:, t, :], i)
                elif name == "skT":
                    pe.wait_ge(ld_sk, 32)
                    transposes(key, sk_nat.rearrange("p h x -> p (h x)"), i)
                elif name == "bias":
                    pe.wait_ge(ld_rel, 32)
                    bank = a_job(key)
                    nc.tensor.matmul(bank[0:NH, 0:FDIST], relb[:, :], onehot, start=True, stop=True)\
                        .then_inc(a_full, 1)
                elif name == "mK":
                    w = weights("w_xk", t)
                    pe.wait_ge(v_free, VN[("memT", 1, 1)] + 1)
                    bank = a_job(key)
                    for c in range(2):
                        cc = (2 * i + c) * P
                        ins = product(bank, c * M, M, lambda k: w[:, k, cc:cc + P], lambda k: K[:, :, k, :])
                    ins.then_inc(a_full, 1)
                elif name == "mV":
                    w = weights("w_xv", t)
                    bank = a_job(key)
                    product(bank, 0, BLK, lambda k: MEMT[i][:, k, :], lambda k: w[:, k, :]).then_inc(a_full, 1)
                elif name == "forget":
                    pe.wait_ge(v_free, VN[("hT", 1, 1)] + 1)
                    pe.wait_ge(ld_wf, 32)
                    bank = v_job(key)
                    product(bank[0:NH, :], 0, SEQ, lambda k: wf[:, k, :], h_both).then_inc(v_full, 1)
                elif name in ("winv", "wina"):
                    w = weights("w_in", t)
                    pe.wait_ge(v_free, VN[("hT", 1, 1)] + 1)
                    bank, full = (v_job(key), v_full) if name == "winv" else (a_job(key), a_full)
                    if t in (2, 5):
                        ins = product(bank, 0, BLK, lambda k: HT[i][:, k, :], lambda k: w[:, k, :])
                    else:
                        for c in range(2):
                            cc = (2 * i + c) * P
                            ins = product(bank, c * SEQ, SEQ, lambda k: w[:, k, cc:cc + P], h_both)
                    ins.then_inc(full, 1)
                elif name == "S":
                    if SN[(t, i)] == 0:
                        pe.wait_ge(a_free, AN[("wina", 5, 1)] + 1)
                        pe.wait_ge(v_free, VN[("winv", 5, 0)] + 1)
                        pe.wait_ge(nc_ready, 1)
                        pe.wait_ge(sel_ready, 1)
                    nk = (t + 1) * P
                    bank = v_job(key)
                    lo, c = (i % 2) * HD, i // 2
                    ins = nc.tensor.matmul(bank[:, 0:nk], Q[lo:lo + HD, t, c, :], K[lo:lo + HD, 0:t + 1, c, :],
                                           start=True, stop=i < NH)
                    if i >= NH:
                        ins = nc.tensor.matmul(bank[:, 0:nk], sel[0:NH, (i - NH) * P:(i - NH + 1) * P],
                                               small[:, 1, 0:nk], start=False, stop=True)
                    ins.then_inc(v_full, 1)
                elif name == "PT":
                    n = SN[(t, i)]
                    pe.wait_ge(p_ready, n + 1)
                    bank = a_job(key)
                    for j in range(t + 1):
                        ins = nc.tensor.transpose(bank[:, j * P:(j + 1) * P], Pr[:, n % 2, j * P:(j + 1) * P],
                                                  ident[:, :])
                    ins.then_inc(a_full, 1)
                elif name == "O":
                    n = SN[(t, i)]
                    pe.wait_ge(a_free, AN[("PT", t, i)] + 1)
                    if t and i % NH == 0:
                        pe.wait_ge(o_raw, 2 * (t - 1) + i // NH + 1)
                    for j in range(t + 1):
                        ins = nc.tensor.matmul(y[:, i * HD:(i + 1) * HD], PT[:, n % 2, j * P:(j + 1) * P],
                                               V[:, j, i * HD:(i + 1) * HD], start=(j == 0), stop=(j == t))
                    if i % NH == NH - 1:
                        ins.then_inc(o_full, 1)
                elif name == "oT":
                    pe.wait_ge(xs_done, XN[("o_scale", t, 0)])
                    transposes(key, HTpage[t], i)
                elif name == "wout":
                    w = weights("w_out", i)
                    pe.wait_ge(v_free, VN[("oT", t, 1)] + 1)
                    bank = v_job(key)
                    product(bank, 0, BLK, lambda k: Q[:, t, k, :], lambda k: w[:, k, :]).then_inc(v_full, 1)
                elif name == "xT":
                    pe.wait_ge(xs_done, XN[("scale_x", t, 0)])
                    transposes(key, XS, i)
                elif name == "xq":
                    w = weights("w_xq", i)
                    pe.wait_ge(v_free, VN[("xT", t, 1)] + 1)
                    bank = a_job(key)
                    for c in range(4):
                        ins = product(bank, c * P, P, lambda k: w[:, k, c * P:(c + 1) * P], lambda k: HT[t][:, k, :])
                    ins.then_inc(a_full, 1)
                elif name == "xS":
                    pe.wait_ge(a_free, AN[("xq", t, 1)] + 1)
                    bank = a_job(key)
                    product(bank, 0, M, lambda j: XQ[:, 2 * i + j, :], lambda j: KM[:, 2 * i + j, :], 2)\
                        .then_inc(a_full, 1)
                elif name == "xPT":
                    n = t * XH_N + i
                    pe.wait_ge(xp, n + 1)
                    bank = a_job(key)
                    for j in range(2):
                        ins = nc.tensor.transpose(bank[:, j * P:(j + 1) * P], Pr[:, n % 2, j * P:(j + 1) * P],
                                                  ident[:, :])
                    ins.then_inc(a_full, 1)
                elif name == "xO":
                    pe.wait_ge(a_free, AN[("xPT", t, i)] + 1)
                    bank = v_job(key)
                    for c in range(2):
                        cc = i * XHD + c * P
                        ins = product(bank, c * P, P, lambda j: VM[:, j, cc:cc + P],
                                      lambda j: PT[:, i % 2, j * P:(j + 1) * P], 2)
                    ins.then_inc(v_full, 1)
                elif name == "xo":
                    w = weights("w_xo", i)
                    pe.wait_ge(v_free, VN[("xO", t, XH_N - 1)] + 1)
                    bank = v_job(key)
                    product(bank, 0, BLK, lambda k: XQ[:, k, :], lambda k: w[:, k, :]).then_inc(v_full, 1)
                elif name == "pT":
                    pe.wait_ge(xs_done, XN[("scale_p", t, 0)])
                    transposes(key, XS, i)
                elif name == "y_start":
                    y_start(t)
                elif name == "wq":
                    w = weights("w_peer_query", i)
                    pe.wait_ge(v_free, VN[("pT", t, 1)] + 1)
                    bank = a_job(key)
                    for c in range(4):
                        ins = product(bank, c * P, P, lambda k: w[:, k, c * P:(c + 1) * P], lambda k: HT[t][:, k, :])
                    ins.then_inc(a_full, 1)
                elif name == "sc":
                    pe.wait_ge(a_free, AN[("wq", t, 1)] + 1)
                    bank = a_job(key)
                    quad, lo = i // 2, (i % 2) * HD
                    for hh in range(4):
                        h = 4 * quad + hh
                        ins = nc.tensor.matmul(bank[:, hh * NKEY:(hh + 1) * NKEY], QR[t][lo:lo + HD, h, :],
                                               skT[lo:lo + HD, h, :], start=True, stop=True)
                    ins.then_inc(a_full, 1)

            def y_start(t):
                for b in range(2):
                    nc.tensor.matmul(y[:, b * BLK:(b + 1) * BLK], ident[:, :], X[t][:, b * BLK:(b + 1) * BLK],
                                     start=True, stop=False)

            def group(g, par, before, last=False):
                pe.wait_ge(diag_done, g + 1)
                for u in range(U):
                    pe.wait_ge(up_in[par * U + u], (before + 1) * 16)
                    for b in range(2):
                        ins = nc.tensor.matmul(y[:, b * BLK:(b + 1) * BLK], diag[:, par, u, :],
                                               UPB[par * U + u][:, b * BLK:(b + 1) * BLK], start=False,
                                               stop=last and u == U - 1)
                ins.then_inc(up_used, 1)

            for st in main:
                step(*st)
            for g in range(GPT):
                group(*flat_group(g // GPH, g % GPH), last=g == GPT - 1)
                for st in after_group(g, True):
                    step(*st)
            pe.wait_ge(y_out, 1)
            y_start(1)
            with pe.Fori(LOOP_LO, LOOP_HI) as m:
                for j in range(3):
                    for k in range(GPH):
                        group(*loop_group(m, j, k))
            for H in (2 * PH - 2, 2 * PH - 1):
                for k in range(GPH):
                    group(*flat_group(H, k), last=H * GPH + k == T * GPT - 1)


INPUTS = ["x", "mem", "norm_mix", "w_in", "b_forget", "rel_bias", "g_moba_out", "g_fox_out", "w_out", "norm_xattn",
          "norm_mem", "w_xq", "w_xk", "w_xv", "w_xo", "norm_ffn", "w_peer_query", "peer_subkeys_1",
          "peer_subkeys_2", "peer_expert_down", "peer_expert_up", "norm_final"]


def kernel(**inputs):
    import concourse.bacc as bacc
    from concourse.bass_utils import run_bass_kernel_spmd as run

    nc = bacc.Bacc("TRN2", target_bir_lowering=False, num_devices=1)
    arrays, aps = {}, {}
    for name in INPUTS:
        arrays[f"in_{name}"] = np.ascontiguousarray(inputs[name])
    arrays["in_bucket_rows"] = bucket_rows()
    for key, a in arrays.items():
        aps[key[3:]] = nc.dram_tensor(key, a.shape, mybir.dt.from_np(a.dtype), kind="ExternalInput").ap()
    out = nc.dram_tensor("out", (1, SEQ, D), mybir.dt.float32, kind="ExternalOutput").ap()
    bias_scratch = nc.dram_tensor("bias_scratch", (NH, P, FDIST), mybir.dt.float32).ap()
    hybrid_layer(nc, aps, out, bias_scratch)
    r = run(nc, [arrays], core_ids=[0])
    return r.results[0]["out"]
```

```python
import math
from contextlib import ExitStack

import numpy as np
import concourse.bass as bass
from concourse import mybir

P = 128
D = 1024
SEQ = 256
T = SEQ // P
M = 256
KC = D // P
HD = 64
NH = 8
BLK = 512
XH_N, XHD = 4, 256
PH, PK = 8, 16
NKEY = 128
N_BUCKETS, MAX_DISTANCE = 32, 128
EPS = 1e-6
NEG = -1e30
W_SLOTS = 6
HC = BLK // 2
U = 2
DEPTH = 3
GPH = PK // U
GPT = PH * GPH
FDIST = 384


def bucket_rows():
    max_exact = N_BUCKETS // 2
    rows = np.zeros((N_BUCKETS + 1, FDIST), np.float32)
    for m in range(FDIST):
        d = (SEQ - 1) - m
        if d < 0:
            rows[N_BUCKETS, m] = NEG
            continue
        b = d
        if d >= max_exact:
            b = min(max_exact + int(math.log(d / max_exact) / math.log(MAX_DISTANCE / max_exact)
                                    * (N_BUCKETS - max_exact)), N_BUCKETS - 1)
        rows[b, m] = 1.0
    return rows


def hybrid_layer(nc, A, out, bias_scratch):
    f32, i32, u32, f32r = mybir.dt.float32, mybir.dt.int32, mybir.dt.uint32, mybir.dt.float32r
    ALU, ACT, AX = mybir.AluOpType, mybir.ActivationFunctionType, mybir.AxisListType

    down_rows = A["peer_expert_down"].rearrange("l e d -> (l e) d")
    up_rows = A["peer_expert_up"].rearrange("l e d -> (l e) d")

    blocks = []
    for name, cols in (("w_xk", 2), ("w_xv", 2), ("w_in", 6), ("w_out", 2), ("w_xq", 2), ("w_xo", 2),
                       ("w_peer_query", 2)):
        blocks += [(name, b) for b in range(cols)]
    BN = {key: n for n, key in enumerate(blocks)}
    halves = [(name, b, i) for name, b in blocks if name in ("w_xk", "w_xv", "w_in") for i in range(2)]
    HN = {key: q for q, key in enumerate(halves)}

    def heads(t, lo, hi):
        out = []
        for h in range(lo, min(lo + 2, hi)):
            out += [("S", t, h)]
        for h in range(lo, hi):
            out += [("PT", t, h)]
            if h + 2 < hi:
                out += [("S", t, h + 2)]
            if h > lo:
                out += [("O", t, h - 1)]
        return out + [("O", t, hi - 1)]

    def xheads(t):
        out = [("xS", t, 0), ("xS", t, 1)]
        for h in range(XH_N):
            out += [("xnorm", t, h), ("xPT", t, h)]
            if h + 2 < XH_N:
                out += [("xS", t, h + 2)]
            if h > 0:
                out += [("xO", t, h - 1)]
        return out + [("xO", t, XH_N - 1)]

    ROOT_AT = 20

    def half_job(q):
        name, b, i = halves[q]
        return {"w_xk": ("mK", b, i), "w_xv": ("mV", b, i), "w_in": ("winv" if i == 0 else "wina", b, i)}[name]

    def projections(lo, hi):
        out = []
        for q in range(lo, hi):
            out += [("split", q + 2, 0)] if q + 2 < len(halves) else []
            out += [half_job(q)]
        return out

    main = [("root_m", 0, 0), ("scale_m", 0, 0), ("root_m", 0, 1), ("scale_m", 0, 1), ("gains", 0, 0),
            ("memT", 0, 0), ("memT", 0, 1), ("memT", 1, 0), ("memT", 1, 1), ("m_parts", 0, 0),
            ("m_parts", 1, 0), ("split", 0, 0), ("split", 1, 0), ("bias", 0, 0), ("root_h", 0, 0), ("root_h", 1, 0),
            ("scale_h", 0, 0), ("scale_h", 1, 0), half_job(0)]
    main += [("hT", t, i) for t in range(T) for i in range(2)] + [("split", 2, 0)] + projections(1, 2)
    main += projections(2, 3) + [("h_parts", 0, 0), ("h_parts", 1, 0), ("f_parts", 0, 0)]
    main += projections(3, 8) + [("forget", 0, 0)]
    main += projections(8, 10) + [("fsum", 0, 0)] + projections(10, len(halves))
    main += heads(0, 0, 2 * NH) + [("o_out", 0, 0), ("o_out", 0, 1), ("o_root", 0, 0), ("o_root", 0, 1)]
    main += [("S", 1, 0), ("S", 1, 1), ("skT", 0, 0), ("skT", 0, 1), ("o_scale", 0, 0)] + heads(1, 0, NH)[2:]
    main += [("oT", 0, 0), ("oT", 0, 1), ("wout", 0, 0), ("wout", 0, 1)]
    fox = heads(1, NH, 2 * NH)
    main += fox[:ROOT_AT] + [("root_x", 0, 0)] + fox[ROOT_AT:ROOT_AT + 6] + [("scale_x", 0, 0)] + fox[ROOT_AT + 6:]
    main += [("o_out", 1, 0), ("o_out", 1, 1), ("o_root", 1, 0), ("o_root", 1, 1)]
    main += [("xT", 0, 0), ("xT", 0, 1), ("xq", 0, 0), ("xq", 0, 1), ("o_scale", 1, 0)]
    xh = xheads(0)
    main += xh[:2] + [("oT", 1, 0), ("oT", 1, 1)] + xh[2:]
    main += [("sqrt_table", 0, 0), ("xo", 0, 0), ("xo", 0, 1), ("root_p", 0, 0), ("wout", 1, 0), ("scale_p", 0, 0),
             ("y_start", 0, 0), ("pT", 0, 0), ("pT", 0, 1), ("start", 0, 0), ("wq_first", 0, 0),
             ("sc_first", 0, 0), ("sc_first", 0, 1), ("top", 0, 0), ("wout", 1, 1), ("wq", 0, 0), ("sc", 0, 0),
             ("sc", 0, 1)]

    slots = [(0, ("wq", 0, 1)), (3, ("sc", 0, 2)), (3, ("sc", 0, 3)),
             (5, ("root_x", 1, 0)), (6, ("scale_x", 1, 0)), (7, ("xT", 1, 0)), (7, ("xT", 1, 1)),
             (10, ("xq", 1, 0)), (13, ("xq", 1, 1))]
    for h in range(XH_N):
        slots += [(17 + 4 * h, ("xS", 1, h)), (20 + 4 * h, ("xnorm", 1, h)), (21 + 4 * h, ("xPT", 1, h)),
                  (24 + 4 * h, ("xO", 1, h))]
    slots += [(39, ("xo", 1, 0)), (42, ("xo", 1, 1)), (44, ("root_p", 1, 0)), (45, ("scale_p", 1, 0)),
              (46, ("pT", 1, 0)), (46, ("pT", 1, 1)), (49, ("wq", 1, 0)), (52, ("sc", 1, 0)), (52, ("sc", 1, 1)),
              (54, ("wq", 1, 1)), (57, ("sc", 1, 2)), (57, ("sc", 1, 3))]
    OWN = ("root_x", "scale_x", "xnorm", "root_p", "scale_p")
    LAG = 2

    def after_group(g, products):
        if products:
            own = [(at, i, st) for i, (at, st) in enumerate(slots) if at == g]
            own.sort(key=lambda e: (e[2][0] in ("xPT",), e[1]))
        else:
            own = [(at, i, st) for i, (at, st) in enumerate(slots)
                   if (at if st[0] in OWN else at + LAG) == g]
            own.sort(key=lambda e: (e[2][0] in ("xPT",), e[1]))
        return [st for _, _, st in own]

    def block_heads(t, b):
        return range(1 if t == 0 and b == 0 else 4 * b, 4 * b + 4)

    TOP_AT = {1: "keys", 2: "sums", 3: "experts"}

    ordered = main + [st for g in range(GPT) for st in after_group(g, True)]
    v_jobs = [st for st in ordered if st[0] in ("gains", "memT", "hT", "forget", "skT", "winv", "S", "oT", "wout",
                                                "xT", "xO", "xo", "pT")]
    a_jobs = [st for st in ordered if st[0] in ("bias", "mK", "mV", "wina", "PT", "xS", "xPT", "xq", "wq", "sc",
                                                "wq_first", "sc_first")]
    VN = {key: n for n, key in enumerate(v_jobs)}
    AN = {key: n for n, key in enumerate(a_jobs)}

    ctx = ExitStack()
    with ctx:
        def sb(name, shape, dt=f32):
            return ctx.enter_context(nc.sbuf_tensor(name, shape, dt))

        def pb(name, shape, dt=f32):
            return ctx.enter_context(nc.psum_tensor(name, shape, dt))

        def sem(name):
            return ctx.enter_context(nc.semaphore(name))

        first = ExitStack()
        with first:
            W_r, SPARE_r, QKVB_r, XH_r, SG_r = [
                first.enter_context(nc.sbuf_tensor(name + "_r", shape, f32r))
                for name, shape in (("weights", [P, W_SLOTS, KC * BLK]), ("spare", [P, 4, D]), ("qkvb", [P, 8, D]),
                                    ("x_and_h", [P, T, 2, D]), ("scaled_gffn", [P, 2, D]))]
        W = sb("weights", [P, W_SLOTS, KC * BLK])
        SPARE = sb("spare", [P, 4, D])
        QKVB = sb("qkvb", [P, 8, D])
        XH = sb("x_and_h", [P, T, 2, D])
        SG = sb("scaled_gffn", [P, 2, D])
        Q = QKVB[:, 0:2, :].rearrange("p t (c x) -> p t c x", c=KC)
        K = QKVB[:, 2:4, :].rearrange("p t (c x) -> p t c x", c=KC)
        V = QKVB[:, 4:6, :]
        B = QKVB[:, 6:8, :].rearrange("p a (h x) -> p (a h) x", h=4)
        X = [XH[:, t, 0, :] for t in range(T)]
        HTpage = [XH[:, t, 1, :] for t in range(T)]
        HT = [h.rearrange("p (c x) -> p c x", c=KC) for h in HTpage]
        KM = sb("mem_k", [P, KC, M])
        VM = sb("mem_v", [P, 2, D])
        XS = SG[:, 0, :]
        XQ = XS[:, :].rearrange("p (c x) -> p c x", c=KC)
        gffn = SG[:, 1, :]
        ident = sb("ident", [P, P])
        FM = sb("fox_mask", [P, SEQ])
        Ssb = sb("s_sb", [P, 2, SEQ])
        Pr = sb("probs", [P, 2, SEQ])
        PT = sb("probs_t", [P, 2, SEQ])
        skT = sb("subkeys_t", [P, PH, NKEY])
        grow = sb("gain_rows", [32, P])
        gcol = sb("gain_cols", [P, 32])
        wf = sb("w_forget", [P, KC, NH])
        wfh = sb("w_forget_high", [P, KC, NH], f32r)
        wfl = sb("w_forget_low", [P, KC, NH], f32r)
        bf = sb("b_forget_col", [NH, 1])
        relb = sb("rel_rows", [N_BUCKETS + 1, NH])
        stat = sb("stat", [P, 16])
        eps = sb("eps", [P, 1])
        nmx = sb("neg_max", [P, 2])
        rsum = sb("row_sum", [P, T, 2 * NH])
        rinv = sb("row_inv", [P, T, 2 * NH])
        xsum = sb("x_sum", [P, 2])
        xinv = sb("x_inv", [P, 2])
        kv = sb("key_vals", [P, 2, PK])
        ku = sb("key_idx", [P, 2, PK], u32)
        kf = sb("key_idx_f", [P, 2, PK])
        tv = sb("top_vals", [P, PK])
        pos = sb("top_pos", [P, PK], u32)
        pab = sb("pos_ab", [P, 2, PK], u32)
        pabf = sb("pos_ab_f", [P, 2, PK])
        hot = sb("one_hot", [P, 2, PK, PK])
        iota16 = sb("iota16", [P, PK])
        picked = sb("picked", [P, 2, PK])
        tneg = sb("top_neg", [P, 1])
        texp = sb("top_exp", [P, PK])
        tsum = sb("top_sum", [P, 1])
        tinv = sb("top_inv", [P, 1])
        IDX = sb("expert_idx", [P, 3, PK])
        GATE = sb("gates", [P, 3, PK])
        ixd = sb("ix_down", [P, DEPTH, U], i32)
        ixu = sb("ix_up", [P, DEPTH, U], i32)
        dots = sb("dots", [P, DEPTH, U])
        gel = sb("gelu", [P, DEPTH, U])
        wgt = sb("wgt", [P, DEPTH, U])
        diag = sb("diag", [P, DEPTH, U, P])
        small = diag[0:NH, :, :, :].rearrange("p a b x -> p a (b x)")
        cand = Ssb[:, 0, :]
        sc = Ssb[:, 1, :].rearrange("p (a x) -> p a x", a=2)

        DN = [QKVB[:, i, :] for i in range(DEPTH * U)]
        UPB = [SPARE[:, i, :] for i in range(4)]
        UPB += [QKVB[:, i, :] for i in (6, 7)]

        wq_early = SPARE[:, :, :].rearrange("p a x -> p (a x)").rearrange("p (k c) -> p k c", k=KC)

        def wslot(name, b):
            return BN[(name, b)] % W_SLOTS

        def wblk(name, b):
            return W[:, wslot(name, b), :].rearrange("p (k c) -> p k c", k=KC)

        SALL = [XH[:, 0, :, :].rearrange("p a x -> p (a x)"), W[:, wslot("w_xq", 1), 0:2 * D]]
        QR = [XS[:, :].rearrange("p (h x) -> p h x", h=PH),
              W[:, wslot("w_xq", 0), 0:D].rearrange("p (h x) -> p h x", h=PH)]
        gfin = W[:, wslot("w_xo", 0), 0:D]
        sk_nat = gffn[:, :].rearrange("p (h x) -> p h x", h=PH)
        brow = Pr[0:NH, :, :].rearrange("p a x -> p (a x)")[:, 0:FDIST]
        onehot = Ssb[0:N_BUCKETS + 1, :, :].rearrange("p a x -> p (a x)")[:, 0:FDIST]
        YS = X

        WH_r = [SPARE_r[:, 2 * i:2 * i + 2, :].rearrange("p a x -> p (a x)").rearrange("p (k c) -> p k c", k=KC)
                for i in range(2)]
        HH_r = SG_r[:, :, :]
        H_whole, HL_r = XH[:, :, 1, :], XH_r[:, :, 1, :]
        MH_r = QKVB_r[:, 0:2, :]
        M_whole, ML_r = QKVB[:, 2:4, :], QKVB_r[:, 2:4, :]

        def half_block(q, of):
            wname, b, half = halves[q]
            return of[:, wslot(wname, b), :].rearrange("p (k c) -> p k c", k=KC)[:, :, half * HC:(half + 1) * HC]

        vb = [pb(f"v_bank{i}", [P, BLK]) for i in range(2)]
        ab = [pb(f"a_bank{i}", [P, BLK]) for i in range(2)]
        y = pb("y", [P, D])
        hp = pb("h_psum", [P, D])

        v_full, v_free = sem("v_full"), sem("v_free")
        a_full, a_free = sem("a_full"), sem("a_free")
        ld_x = [sem(f"ld_x{t}") for t in range(T)]
        ld_early = sem("ld_early")
        ld_mem = [sem(f"ld_mem{m}") for m in range(2)]
        ld_gain, ld_sk, ld_rel, ld_wf, ld_gffn, ld_gfin = (sem("ld_gain"), sem("ld_sk"), sem("ld_rel"),
                                                           sem("ld_wf"), sem("ld_gffn"), sem("ld_gfin"))
        w_full = [sem(f"w_full{i}") for i in range(W_SLOTS)]
        id_ready, fm_ready, rel_one, io_ready = sem("id_ready"), sem("fm_ready"), sem("rel_one"), sem("io_ready")
        pool_ch, eps_ready = sem("pool_ch"), sem("eps_ready")
        sum_done = sem("sum_done")
        sq_done = sem("sq_done")
        xs_done = sem("xs_done")
        brow_out, ld_bias = sem("brow_out"), sem("ld_bias")
        fz, fe, fe1, fl, nc_ready = sem("fz"), sem("fe"), sem("fe1"), sem("fl"), sem("nc_ready")
        high_ready, low_ready = sem("high_ready"), sem("low_ready")
        mh_ready, ml_ready, hh_ready, hl_ready = sem("mh_ready"), sem("ml_ready"), sem("hh_ready"), sem("hl_ready")
        p_ready, o_full = sem("p_ready"), sem("o_full")
        o_raw = sem("o_raw")
        xmax, xp = sem("xmax"), sem("xp")
        top_in, top_exp, idx_ready = sem("top_in"), sem("top_e"), sem("idx_ready")
        go_dn = [sem(f"go_dn{i}") for i in range(DEPTH)]
        go_up = [sem(f"go_up{i}") for i in range(DEPTH)]
        dn_in = [sem(f"dn_in{i}") for i in range(DEPTH * U)]
        up_in = [sem(f"up_in{i}") for i in range(DEPTH * U)]
        dot_done, gelu_done, diag_done, up_used = (sem("dot_done"), sem("gelu_done"), sem("diag_done"),
                                                   sem("up_used"))
        dve_ch = sem("dve_ch")
        w_done, hp_ready, top_ch = sem("w_done"), sem("hp_ready"), sem("top_ch")
        y_out, out_ready, out_done = sem("y_out"), sem("out_ready"), sem("out_done")

        roots = [st for st in ordered if st[0] in ("root_m", "root_h", "o_root", "root_x", "root_p")]
        roots += [("root_y", 0, 0), ("root_y", 1, 0)]
        SQ = {key: n + 1 for n, key in enumerate(roots)}
        scales = [st for st in main + [st for _, st in slots]
                  if st[0] in ("scale_m", "scale_h", "o_scale", "scale_x", "scale_p")]
        XN = {key: n + 1 for n, key in enumerate(scales)}
        SN = {key[1:]: n for n, key in enumerate(st for st in main if st[0] == "S")}

        def col(name, t, i):
            return {"root_m": i, "root_h": 2 + t, "o_root": 4 + 2 * t + i, "root_x": 8 + 2 * t,
                    "root_p": 9 + 2 * t, "root_y": 12 + t}[name]

        MEM = [Q[:, m, :, :].rearrange("p c x -> p (c x)") for m in range(2)]
        MEMT = [K[:, m, :, :] for m in range(2)]

        block = ctx.enter_context(nc.Block())

        def load_gain(engine, r):
            name, lo, n = (("norm_mix", 0, 8), ("g_moba_out", 8, 4), ("g_fox_out", 12, 4), ("norm_xattn", 16, 8),
                           ("norm_mem", 24, 8))[r]
            engine.dma_start(grow[lo:lo + n, :], A[name][0].rearrange("(k p) -> k p", p=P)).then_inc(ld_gain, 16)

        @block.sync
        def _(sp):
            def used_up(name, b):
                if name == "w_out":
                    return v_full, VN[("wout", 1, b)] + 1
                return a_full, AN[({"w_xk": "mK", "w_xv": "mV", "w_in": "wina"}[name], b, 1)] + 1

            def load_block(n):
                name, b = blocks[n]
                if n >= W_SLOTS:
                    sp.wait_ge(*used_up(*blocks[n - W_SLOTS]))
                src = A[name][0].rearrange("(k p) c -> p k c", p=P)[:, :, b * BLK:(b + 1) * BLK]
                sp.dma_start(W[:, n % W_SLOTS, :].rearrange("p (k c) -> p k c", k=KC), src)\
                    .then_inc(w_full[n % W_SLOTS], 16)

            for m in range(2):
                sp.dma_start(QKVB[:, m, :], A["mem"][0, m * P:(m + 1) * P, :]).then_inc(ld_mem[m], 16)
            load_gain(sp, 1)
            load_gain(sp, 2)
            load_block(0)
            for t in range(T):
                sp.dma_start(X[t], A["x"][0, t * P:(t + 1) * P, :]).then_inc(ld_x[t], 16)
            sp.wait_ge(rel_one, 1)
            sp.dma_start(relb[0:N_BUCKETS, :], A["rel_bias"]).then_inc(ld_rel, 16)
            sp.dma_start(onehot, A["bucket_rows"]).then_inc(ld_rel, 16)
            load_block(1)
            sp.dma_start(bf[:, :], A["b_forget"][0].rearrange("(h a) -> h a", a=1)).then_inc(ld_wf, 16)
            sp.dma_start(wf[:, :, :], A["w_in"][0].rearrange("(k p) c -> p k c", p=P)[:, :, 6 * BLK:6 * BLK + NH])\
                .then_inc(ld_wf, 16)
            for n in range(2, W_SLOTS):
                load_block(n)
            sp.wait_ge(a_free, AN[("bias", 0, 0)] + 1)
            sp.dma_start(bias_scratch, brow.unsqueeze(1).broadcast_to([NH, P, FDIST])).then_inc(brow_out, 16)
            load_block(W_SLOTS)
            sp.wait_ge(brow_out, 16)
            for h in range(NH):
                toeplitz = bass.AP(tensor=bias_scratch.tensor, offset=h * P * FDIST + P - 1,
                                   ap=[[FDIST - 1, P], [1, SEQ]])
                sp.dma_start(B[:, h, :], toeplitz).then_inc(ld_bias, 16)
            for n in range(W_SLOTS + 1, len(blocks)):
                if n == BN[("w_peer_query", 0)]:
                    sp.wait_ge(a_full, AN[("wina", 5, 1)] + 1)
                    sp.wait_ge(v_full, VN[("winv", 5, 0)] + 1)
                    sp.dma_start(wq_early, A["w_peer_query"][0].rearrange("(k p) c -> p k c", p=P)[:, :, 0:BLK])\
                        .then_inc(ld_early, 16)
                    for half, name in enumerate(("peer_subkeys_1", "peer_subkeys_2")):
                        sp.dma_start(sk_nat[:, :, half * HD:(half + 1) * HD], A[name][0].rearrange("h n d -> n h d"))\
                            .then_inc(ld_sk, 16)
                    sp.wait_ge(v_full, VN[("skT", 0, 1)] + 1)
                    sp.dma_start(gffn[:, :], A["norm_ffn"][0:1, :].broadcast_to([P, D])).then_inc(ld_gffn, 16)
                load_block(n)
            sp.wait_ge(v_full, VN[("xo", 1, 0)] + 1)
            sp.dma_start(gfin, A["norm_final"].rearrange("(a d) -> a d", a=1).broadcast_to([P, D]))\
                .then_inc(ld_gfin, 16)
            for t in range(T):
                sp.wait_ge(out_ready, t + 1)
                sp.dma_start(out[0, t * P:(t + 1) * P, :], YS[t]).then_inc(out_done, 16)
            sp.wait_ge(out_done, 16 * T)

        @block.gpsimd
        def _(pool):
            def link(ins, n):
                ins.then_inc(pool_ch, 1)
                pool.wait_ge(pool_ch, n)

            link(pool.memset(ident[:], 0.0), 1)
            pool.affine_select(out=ident[:], in_=ident[:], compare_op=ALU.not_equal, fill=1.0, base=0,
                               pattern=[[-1, P]], channel_multiplier=1).then_inc(id_ready, 1)
            pool.memset(relb[:], 1.0).then_inc(rel_one, 1)
            pool.memset(eps[:], EPS).then_inc(eps_ready, 1)
            link(pool.memset(FM[:], 0.0), 2)
            pool.affine_select(out=FM[:], in_=FM[:], compare_op=ALU.is_ge, fill=NEG, base=P,
                               pattern=[[-1, SEQ]], channel_multiplier=1).then_inc(fm_ready, 1)
            pool.iota(iota16[:], [[1, PK]], base=0, channel_multiplier=0,
                      allow_small_or_imprecise_dtypes=True).then_inc(io_ready, 1)
            def group(par):
                pool.wait_ge(go_dn[par], 1)
                pool.sem_clear(go_dn[par])
                for u in range(U):
                    pool.indirect_dma_start(DN[par * U + u], None, down_rows,
                                            bass.IndirectOffsetOnAxis(ap=ixd[:, par, u:u + 1], axis=0))\
                        .then_inc(dn_in[par * U + u], 16)
                pool.wait_ge(go_up[par], 1)
                pool.sem_clear(go_up[par])
                for u in range(U):
                    pool.indirect_dma_start(UPB[par * U + u], None, up_rows,
                                            bass.IndirectOffsetOnAxis(ap=ixu[:, par, u:u + 1], axis=0))\
                        .then_inc(up_in[par * U + u], 16)

            with pool.Fori(0, T * GPT // DEPTH) as i:
                for par in range(DEPTH):
                    group(par)
            for par in range(T * GPT % DEPTH):
                group(par)

        LOOP_LO, LOOP_HI = PH // 3, PH // 3 + (PH - 2) // 3
        assert 3 * LOOP_LO + 2 == PH and 3 * LOOP_HI + 2 == 2 * PH - 2

        def loop_group(m, j, k):
            rest = (2 + j) * GPH + k
            return m * (3 * GPH) + rest, rest % DEPTH, m * GPH + rest // DEPTH

        def flat_group(H, k):
            g = H * GPH + k
            return g, g % DEPTH, g // DEPTH

        @block.scalar
        def _(act):
            for r in (4, 0, 3):
                load_gain(act, r)
            act.wait_ge(eps_ready, 1)
            nc.scalar.activation(stat[:, 15:16], eps[:, 0:1], ACT.Sqrt)

            norm_n = [0]

            def root(key, src, junk, width):
                norm_n[0] += 1
                n = col(*key)
                nc.scalar.activation(junk, src, ACT.Square, accum_out=stat[:, n:n + 1]).then_inc(sum_done, 1)
                act.wait_ge(sum_done, norm_n[0])
                nc.scalar.activation(stat[:, n:n + 1], stat[:, n:n + 1], ACT.Sqrt, bias=eps[:, 0:1],
                                     scale=1.0 / width).then_inc(sq_done, 1)

            def job(key):
                act.wait_ge(a_full, AN[key] + 1)
                return ab[AN[key] % 2]

            def step(name, t, i):
                key = (name, t, i)
                if name == "top":
                    top_softmax(0)
                    act.wait_ge(idx_ready, 1)
                    for g in range(3):
                        stage_down(g)
                    act.wait_ge(a_full, AN[("wq", 0, 0)] + 1)
                    for g in range(2):
                        stage_up(g)
                if name == "root_m":
                    act.wait_ge(ld_mem[i], 16)
                    root(key, MEM[i], V[:, i, :], D)
                elif name == "root_h":
                    act.wait_ge(ld_x[t], 16)
                    act.wait_ge(sq_done, 2)
                    root(key, X[t], V[:, t, :], D)
                elif name == "bias":
                    src = job(key)
                    act.copy(brow, src[0:NH, 0:FDIST]).then_inc(a_free, 1)
                elif name == "mK":
                    src = job(key)
                    act.copy(KM[:, 4 * t + 2 * i:4 * t + 2 * i + 2, :],
                             src[:, :].rearrange("p (c x) -> p c x", c=2)).then_inc(a_free, 1)
                elif name == "mV":
                    src = job(key)
                    act.copy(VM[:, :, t * BLK + i * HC:t * BLK + (i + 1) * HC],
                             src[:, :].rearrange("p (m c) -> p m c", m=2)).then_inc(a_free, 1)
                elif name == "m_parts":
                    act.wait_ge(v_free, VN[("memT", t, 1)] + 1)
                    act.copy(MH_r[:, t, :], M_whole[:, t, :]).then_inc(mh_ready, 1)
                elif name == "h_parts":
                    act.wait_ge(v_free, VN[("hT", t, 1)] + 1)
                    act.copy(HH_r[:, t, :], H_whole[:, t, :]).then_inc(hh_ready, 1)
                elif name == "split":
                    wname, b, half = halves[t]
                    n = BN[(wname, b)]
                    act.wait_ge(w_full[n % W_SLOTS], 16 * (n // W_SLOTS + 1))
                    if t >= 2:
                        used = half_job(t - 2)
                        act.wait_ge(v_full if used[0] == "winv" else a_full,
                                    (VN if used[0] == "winv" else AN)[used] + 1)
                    act.copy(WH_r[t % 2], half_block(t, W)).then_inc(high_ready, 1)
                elif name == "sqrt_table":
                    nc.scalar.activation(stat[:, 15:16], eps[:, 0:1], ACT.Sqrt)
                elif name == "f_parts":
                    act.wait_ge(ld_wf, 32)
                    act.copy(wfh[:, :, :], wf[:, :, :]).then_inc(hh_ready, 1)
                elif name == "fsum":
                    act.wait_ge(fz, 1)
                    nc.scalar.activation(small[:, 2, :], small[:, 2, :], ACT.Exp).then_inc(fe, 1)
                    act.wait_ge(fe1, 1)
                    nc.scalar.activation(small[:, 2, :], small[:, 2, :], ACT.Ln).then_inc(fl, 1)
                elif name == "wina":
                    src, b = job(key), t
                    if b in (2, 5):
                        act.copy(V[:, :, (b // 3) * BLK + HC:(b // 3 + 1) * BLK],
                                 src[:, :].rearrange("p (t c) -> p t c", t=T)).then_inc(a_free, 1)
                    else:
                        dst = (Q if b % 3 == 0 else K)[:, :, (b // 3) * 4 + 2:(b // 3) * 4 + 4, :]
                        act.mul(dst.rearrange("p t c x -> p c t x"),
                                src[:, :].rearrange("p (c t x) -> p c t x", c=2, t=2),
                                HD ** -0.5 if b % 3 == 0 else 1.0).then_inc(a_free, 1)
                elif name == "S":
                    n, nk = SN[(t, i)], (t + 1) * P
                    act.wait_ge(v_free, VN[key] + 1)
                    if n >= 2:
                        prev = [k for k, v in SN.items() if v == n - 2][0]
                        act.wait_ge(a_full, AN[("PT",) + prev] + 1)
                    nc.scalar.activation(Pr[:, n % 2, 0:nk], Ssb[:, n % 2, 0:nk], ACT.Exp,
                                         bias=nmx[:, n % 2:n % 2 + 1], scale=-1.0,
                                         accum_out=rsum[:, t, i:i + 1]).then_inc(p_ready, 1)
                elif name == "PT":
                    src, n, nk = job(key), SN[(t, i)], (t + 1) * P
                    act.copy(PT[:, n % 2, 0:nk], src[:, 0:nk]).then_inc(a_free, 1)
                elif name == "o_root":
                    act.wait_ge(o_raw, 2 * t + i + 1)
                    root(key, HTpage[t][:, i * BLK:(i + 1) * BLK], QKVB[:, t, i * BLK:(i + 1) * BLK], BLK)
                elif name == "root_x":
                    act.wait_ge(v_free, VN[("wout", t, 1)] + 1)
                    root(key, X[t], XS[:, :], D)
                elif name == "xq":
                    src = job(key)
                    act.mul(XQ[:, 4 * i:4 * i + 4, :], src[:, :].rearrange("p (c x) -> p c x", c=4),
                            XHD ** -0.5).then_inc(a_free, 1)
                elif name == "xS":
                    n = t * XH_N + i
                    src = job(key)
                    act.wait_ge(xmax, n + 1)
                    nc.scalar.activation(Pr[:, n % 2, :], src[:, 0:M], ACT.Exp, bias=nmx[:, n % 2:n % 2 + 1],
                                         accum_out=xsum[:, n % 2:n % 2 + 1]).then_inc(a_free, 1)
                elif name == "xPT":
                    src = job(key)
                    act.copy(PT[:, i % 2, :], src[:, 0:M]).then_inc(a_free, 1)
                elif name == "root_p":
                    act.wait_ge(v_free, VN[("xo", t, 1)] + 1)
                    root(key, X[t], XS[:, :], D)
                elif name in ("wq", "wq_first"):
                    src = job(key)
                    if t == 0:
                        act.wait_ge(hp_ready, 1)
                    hs = block_heads(t, i) if name == "wq" else range(1)
                    lo, hi = hs[0], hs[-1] + 1
                    act.copy(QR[t][:, lo:hi, :], src[:, (lo - 4 * i) * P:(hi - 4 * i) * P]
                             .rearrange("p (c x) -> p c x", x=P)).then_inc(a_free, 1)
                elif name in ("sc", "sc_first"):
                    src = job(key)
                    dst = SALL[t].rearrange("p (h s x) -> p h s x", s=2, x=NKEY)
                    b = i // 2
                    hs = block_heads(t, b) if name == "sc" else range(1)
                    lo, hi = hs[0], hs[-1] + 1
                    act.copy(dst[:, lo:hi, i % 2, :], src[:, (lo - 4 * b) * NKEY:(hi - 4 * b) * NKEY]
                             .rearrange("p (h x) -> p h x", x=NKEY)).then_inc(a_free, 1)

            def top_softmax(H):
                act.wait_ge(top_in, H + 1)
                nc.scalar.activation(texp[:], tv[:], ACT.Exp, bias=tneg[:, 0:1], accum_out=tsum[:, 0:1])\
                    .then_inc(top_exp, 1)

            def stage_down(rest):
                par, H3, k = rest % DEPTH, rest // GPH % 3, rest % GPH
                nc.scalar.activation(ixd[:, par, :], IDX[:, H3, k * U:(k + 1) * U], ACT.Copy)\
                    .then_inc(go_dn[par], 1)

            def stage_up(rest):
                par, H3, k = rest % DEPTH, rest // GPH % 3, rest % GPH
                nc.scalar.activation(ixu[:, par, :], IDX[:, H3, k * U:(k + 1) * U], ACT.Copy)\
                    .then_inc(go_up[par], 1)

            def group(H, g, rest, left=GPT):
                par, k = rest % DEPTH, rest % GPH
                act.wait_ge(dot_done, (g + 1) * U)
                nc.scalar.activation(gel[:, par, :], dots[:, par, :], ACT.Gelu).then_inc(gelu_done, 1)
                if left >= 3:
                    if k == GPH - 3:
                        act.wait_ge(idx_ready, H + 2)
                    stage_down(rest + 3)
                if left >= 2:
                    if not isinstance(g, int) or g >= 1:
                        act.wait_ge(up_used, g)
                    stage_up(rest + 2)

            for st in main:
                step(*st)
            for g in range(GPT):
                group(g // GPH, g, g)
                for st in after_group(g, False):
                    step(*st)
                if TOP_AT.get(g % GPH) == "sums":
                    top_softmax(g // GPH + 1)
            act.wait_ge(y_out, 1)
            root(("root_y", 0, 0), YS[0], HTpage[0], D)
            with act.Fori(LOOP_LO, LOOP_HI) as m:
                for j in range(3):
                    for k in range(GPH):
                        group(m * 3 + (2 + j), loop_group(m, j, k)[0], (2 + j) * GPH + k)
                        if TOP_AT.get(k) == "sums":
                            top_softmax(m * 3 + (3 + j))
            for H in (2 * PH - 2, 2 * PH - 1):
                for k in range(GPH):
                    g = H * GPH + k
                    group(H, g, g, left=T * GPT - 1 - g)
                    if TOP_AT.get(k) == "sums" and H < 2 * PH - 1:
                        top_softmax(H + 1)
            nc.scalar.activation(stat[:, 15:16], eps[:, 0:1], ACT.Sqrt)
            act.wait_ge(up_used, T * GPT)
            root(("root_y", 1, 0), y[:, :], HTpage[1], D)

        @block.vector
        def _(dve):
            chain = [0]

            def link(ins):
                ins.then_inc(dve_ch, 1)
                chain[0] += 1
                dve.wait_ge(dve_ch, chain[0])

            def job(key):
                dve.wait_ge(v_full, VN[key] + 1)
                return vb[VN[key] % 2]

            def rstd(key):
                dve.wait_ge(sq_done, SQ[key])
                c = col(*key)
                link(nc.vector.reciprocal(stat[:, c:c + 1], stat[:, c:c + 1]))
                return stat[:, c:c + 1]

            def gained(key, half, dst, c0):
                src = job(key)
                gain = gcol[:, c0 + 4 * half:c0 + 4 * half + 4].unsqueeze(2).broadcast_to([P, 4, P])
                nc.vector.tensor_tensor(dst[:, 4 * half:4 * half + 4, :],
                                        src[:, :].rearrange("p (c x) -> p c x", c=4),
                                        gain, ALU.mult).then_inc(v_free, 1)

            def step(name, t, i):
                key = (name, t, i)
                if name == "start":
                    start_tile(0)
                elif name == "top":
                    dve.wait_ge(io_ready, 1)
                    dve.wait_ge(a_free, AN[("sc_first", 0, 1)] + 1)
                    for part in TOP_AT.values():
                        top_part(part, 0, 0, static_scores(0))
                if name == "gains":
                    src = job(key)
                    nc.vector.tensor_copy(gcol[:, :], src[:, 0:32]).then_inc(v_free, 1)
                    dve.wait_ge(v_free, VN[key] + 1)
                elif name == "scale_m":
                    r = rstd(("root_m", 0, i))
                    nc.vector.tensor_scalar(MEM[i], MEM[i], r, None, ALU.mult).then_inc(xs_done, 1)
                elif name == "scale_h":
                    r = rstd(("root_h", t, 0))
                    nc.vector.tensor_scalar(V[:, t, :], X[t], r, None, ALU.mult).then_inc(xs_done, 1)
                elif name == "memT":
                    gained(key, i, MEMT[t], 24)
                elif name == "hT":
                    gained(key, i, HT[t], 0)
                elif name == "m_parts":
                    dve.wait_ge(mh_ready, t + 1)
                    nc.vector.tensor_tensor(ML_r[:, t, :], M_whole[:, t, :], MH_r[:, t, :].bitcast(f32),
                                            ALU.subtract).then_inc(ml_ready, 1)
                elif name == "h_parts":
                    dve.wait_ge(hh_ready, t + 1)
                    nc.vector.tensor_tensor(HL_r[:, t, :], H_whole[:, t, :], HH_r[:, t, :].bitcast(f32),
                                            ALU.subtract).then_inc(hl_ready, 1)
                elif name == "f_parts":
                    dve.wait_ge(hh_ready, T + 1)
                    nc.vector.tensor_tensor(wfl[:, :, :], wf[:, :, :], wfh[:, :, :].bitcast(f32), ALU.subtract)\
                        .then_inc(hl_ready, 1)
                elif name == "split":
                    dve.wait_ge(high_ready, t + 1)
                    nc.vector.tensor_tensor(half_block(t, W_r), half_block(t, W), WH_r[t % 2].bitcast(f32),
                                            ALU.subtract).then_inc(low_ready, 1)
                elif name == "skT":
                    src = job(key)
                    nc.vector.tensor_copy(skT[:, 4 * i:4 * i + 4, :], src[:, :].rearrange("p (c x) -> p c x", c=4))\
                        .then_inc(v_free, 1)
                elif name == "forget":
                    src = job(key)
                    nc.vector.tensor_scalar(small[:, 0, :], src[0:NH, 0:SEQ], bf[:, 0:1], None, ALU.add)\
                        .then_inc(v_free, 1)
                    dve.wait_ge(v_free, VN[key] + 1)
                    link(nc.vector.tensor_scalar(small[:, 1, :], small[:, 0, :], 0.0, None, ALU.min))
                    nc.vector.scalar_tensor_tensor(out=small[:, 2, :], in0=small[:, 1, :], scalar=2.0,
                                                   in1=small[:, 0, :], op0=ALU.mult, op1=ALU.subtract)\
                        .then_inc(fz, 1)
                elif name == "fsum":
                    dve.wait_ge(fe, 1)
                    nc.vector.tensor_scalar(small[:, 2, :], small[:, 2, :], 1.0, None, ALU.add).then_inc(fe1, 1)
                    dve.wait_ge(fl, 1)
                    link(nc.vector.tensor_tensor(small[:, 0, :], small[:, 2, :], small[:, 1, :], ALU.subtract))
                    nc.vector.tensor_tensor_scan(small[:, 1, :], small[:, 0, :], small[:, 0, :], 0.0,
                                                 ALU.add, ALU.bypass).then_inc(nc_ready, 1)
                elif name == "winv":
                    src, b = job(key), t
                    if b in (2, 5):
                        nc.vector.tensor_copy(V[:, :, (b // 3) * BLK:(b // 3) * BLK + HC],
                                              src[:, :].rearrange("p (t c) -> p t c", t=T)).then_inc(v_free, 1)
                    else:
                        dst = (Q if b % 3 == 0 else K)[:, :, (b // 3) * 4:(b // 3) * 4 + 2, :]
                        nc.vector.tensor_scalar(dst.rearrange("p t c x -> p c t x"),
                                                src[:, :].rearrange("p (c t x) -> p c t x", c=2, t=2),
                                                HD ** -0.5 if b % 3 == 0 else 1.0, None, ALU.mult)\
                            .then_inc(v_free, 1)
                elif name == "S":
                    n, nk = SN[(t, i)], (t + 1) * P
                    src = job(key)
                    if n == 0:
                        dve.wait_ge(ld_bias, 16 * NH)
                        dve.wait_ge(fm_ready, 1)
                    if n >= 2:
                        dve.wait_ge(p_ready, n - 1)
                    add = B[:, i, SEQ - nk:SEQ] if i < NH else FM[:, SEQ - nk:SEQ]
                    nc.vector.tensor_tensor_reduce(out=Ssb[:, n % 2, 0:nk], in0=src[:, 0:nk], in1=add,
                                                   scale=-1.0, scalar=3e38, op0=ALU.add, op1=ALU.min,
                                                   accum_out=nmx[:, n % 2:n % 2 + 1]).then_inc(v_free, 1)
                elif name == "o_out":
                    if i == 0:
                        dve.wait_ge(p_ready, SN[(t, 2 * NH - 1)] + 1)
                        link(nc.vector.reciprocal(rinv[:, t, :], rsum[:, t, :]))
                    dve.wait_ge(o_full, 2 * t + i + 1)
                    nc.vector.tensor_tensor(
                        HTpage[t][:, i * BLK:(i + 1) * BLK].rearrange("p (h x) -> p h x", h=NH),
                        y[:, i * BLK:(i + 1) * BLK].rearrange("p (h x) -> p h x", h=NH),
                        rinv[:, t, i * NH:(i + 1) * NH].unsqueeze(2).broadcast_to([P, NH, HD]),
                        ALU.mult).then_inc(o_raw, 1)
                elif name == "o_scale":
                    for g in range(2):
                        r = rstd(("o_root", t, g))
                        part = HTpage[t][:, g * BLK:(g + 1) * BLK]
                        ins = nc.vector.tensor_scalar(part, part, r, None, ALU.mult)
                        if g == 0:
                            link(ins)
                        else:
                            ins.then_inc(xs_done, 1)
                elif name == "oT":
                    gained(key, i, HT[t], 8)
                elif name in ("wout", "xo"):
                    src = job(key)
                    part = X[t][:, i * BLK:(i + 1) * BLK]
                    nc.vector.tensor_tensor(part, src[:, :], part, ALU.add).then_inc(v_free, 1)
                elif name == "scale_x":
                    r = rstd(("root_x", t, 0))
                    nc.vector.tensor_scalar(XS[:, :], X[t], r, None, ALU.mult).then_inc(xs_done, 1)
                elif name == "xT":
                    gained(key, i, HT[t], 16)
                elif name == "xS":
                    n = t * XH_N + i
                    dve.wait_ge(a_full, AN[key] + 1)
                    nc.vector.tensor_reduce(nmx[:, n % 2:n % 2 + 1], ab[AN[key] % 2][:, 0:M], AX.X,
                                            ALU.max, negate=True).then_inc(xmax, 1)
                elif name == "xnorm":
                    n = t * XH_N + i
                    dve.wait_ge(a_free, AN[("xS", t, i)] + 1)
                    link(nc.vector.reciprocal(xinv[:, n % 2:n % 2 + 1], xsum[:, n % 2:n % 2 + 1]))
                    nc.vector.tensor_scalar(Pr[:, n % 2, :], Pr[:, n % 2, :], xinv[:, n % 2:n % 2 + 1], None,
                                            ALU.mult).then_inc(xp, 1)
                elif name == "xO":
                    src = job(key)
                    nc.vector.tensor_copy(XQ[:, 2 * i:2 * i + 2, :],
                                          src[:, 0:2 * P].rearrange("p (c x) -> p c x", c=2)).then_inc(v_free, 1)
                elif name == "scale_p":
                    r = rstd(("root_p", t, 0))
                    dve.wait_ge(ld_gffn, 16)
                    nc.vector.scalar_tensor_tensor(out=XS[:, :], in0=X[t], scalar=r, in1=gffn[:, :],
                                                   op0=ALU.mult, op1=ALU.mult).then_inc(xs_done, 1)
                elif name == "pT":
                    src = job(key)
                    nc.vector.tensor_copy(HT[t][:, 4 * i:4 * i + 4, :],
                                          src[:, :].rearrange("p (c x) -> p c x", c=4)).then_inc(v_free, 1)

            top_n = [0]

            def t_mark(ins):
                ins.then_inc(top_ch, 1)
                top_n[0] += 1
                return top_n[0]

            def after(k):
                dve.wait_ge(top_ch, k)

            def top_keys(scores):
                top_n[0] = 0
                after(t_mark(nc.vector.tensor_copy(sc[:, :, :].rearrange("p a x -> p (a x)"), scores)))
                for rnd in range(2):
                    lo = 8 * rnd
                    m = [t_mark(nc.vector.max(kv[:, s, lo:lo + 8], sc[:, s, :])) for s in range(2)]
                    for s in range(2):
                        after(m[s])
                        last = t_mark(nc.vector.max_index(ku[:, s, lo:lo + 8], kv[:, s, lo:lo + 8], sc[:, s, :]))
                    if rnd == 0:
                        for s in range(2):
                            last = t_mark(nc.vector.match_replace(sc[:, s, :], kv[:, s, 0:8], sc[:, s, :], -3e38))
                    after(last)
                t_mark(nc.vector.tensor_copy(kf[:, :, :], ku[:, :, :]))
                cv = cand[:, :].rearrange("p (a b) -> p a b", a=PK)
                after(t_mark(nc.vector.tensor_tensor(cv, kv[:, 0, :].unsqueeze(2).broadcast_to([P, PK, PK]),
                                                     kv[:, 1, :].unsqueeze(1).broadcast_to([P, PK, PK]), ALU.add)))

            def top_sums():
                for rnd in range(2):
                    lo = 8 * rnd
                    after(t_mark(nc.vector.max(tv[:, lo:lo + 8], cand[:, :])))
                    last = t_mark(nc.vector.max_index(pos[:, lo:lo + 8], tv[:, lo:lo + 8], cand[:, :]))
                    if rnd == 0:
                        last = t_mark(nc.vector.match_replace(cand[:, :], tv[:, 0:8], cand[:, :], -3e38))
                    after(last)
                nc.vector.tensor_scalar(tneg[:, 0:1], tv[:, 0:1], -1.0, None, ALU.mult).then_inc(top_in, 1)

            def top_experts(H, H3):
                t_mark(nc.vector.tensor_scalar(pab[:, 0, :], pos[:, :], 4, None, ALU.logical_shift_right))
                after(t_mark(nc.vector.tensor_scalar(pab[:, 1, :], pos[:, :], 15, None, ALU.bitwise_and)))
                after(t_mark(nc.vector.tensor_copy(pabf[:, :, :], pab[:, :, :])))
                for s in range(2):
                    last = t_mark(nc.vector.tensor_tensor(
                        hot[:, s, :, :], pabf[:, s, :].unsqueeze(2).broadcast_to([P, PK, PK]),
                        iota16[:, :].unsqueeze(1).broadcast_to([P, PK, PK]), ALU.is_equal))
                after(last)
                for s in range(2):
                    last = t_mark(nc.vector.tensor_tensor(
                        hot[:, s, :, :], hot[:, s, :, :],
                        kf[:, s, :].unsqueeze(1).broadcast_to([P, PK, PK]), ALU.mult))
                after(last)
                after(t_mark(nc.vector.tensor_reduce(picked[:, :, :], hot[:, :, :, :], AX.X, ALU.add)))
                nc.vector.scalar_tensor_tensor(out=IDX[:, H3, :], in0=picked[:, 0, :], scalar=float(NKEY),
                                               in1=picked[:, 1, :], op0=ALU.mult, op1=ALU.add).then_inc(idx_ready, 1)
                dve.wait_ge(top_exp, H + 1)
                after(t_mark(nc.vector.reciprocal(tinv[:, :], tsum[:, :])))
                after(t_mark(nc.vector.tensor_scalar(GATE[:, H3, :], texp[:, :], tinv[:, 0:1], None, ALU.mult)))
                dve.sem_clear(top_ch)

            def top_part(part, H, H3, scores):
                if part == "keys":
                    top_keys(scores)
                elif part == "sums":
                    top_sums()
                elif part == "experts":
                    top_experts(H, H3)

            def static_scores(H):
                return SALL[H // PH][:, (H % PH) * 2 * NKEY:(H % PH + 1) * 2 * NKEY]

            def group(H3, k, g, par, before):
                for u in range(U):
                    dve.wait_ge(dn_in[par * U + u], (before + 1) * 16)
                    ins = nc.vector.tensor_tensor_reduce(out=DN[par * U + u], in0=hp[:, :], in1=DN[par * U + u],
                                                         scale=1.0, scalar=0.0, op0=ALU.mult, op1=ALU.add,
                                                         accum_out=dots[:, par, u:u + 1])
                    ins.then_inc(dot_done, 1)
                dve.wait_ge(gelu_done, g + 1)
                nc.vector.tensor_tensor(wgt[:, par, :], gel[:, par, :], GATE[:, H3, k * U:(k + 1) * U],
                                        ALU.mult).then_inc(w_done, 1)
                dve.wait_ge(w_done, g + 1)
                if not isinstance(g, int) or g >= 3:
                    dve.wait_ge(up_used, g - 2)
                for u in range(U):
                    ins = nc.vector.tensor_scalar(diag[:, par, u, :], ident[:, :], wgt[:, par, u:u + 1], None, ALU.mult)
                ins.then_inc(diag_done, 1)

            def start_tile(t):
                nc.vector.tensor_copy(hp[:, :], XS[:, :]).then_inc(hp_ready, 1)
                dve.wait_ge(hp_ready, t + 1)

            def finish(t, rows):
                r = rstd(("root_y", t, 0))
                dve.wait_ge(ld_gfin, 16)
                nc.vector.scalar_tensor_tensor(out=YS[t], in0=rows, scalar=r, in1=gfin,
                                               op0=ALU.mult, op1=ALU.mult).then_inc(out_ready, 1)

            for st in main:
                step(*st)
            scores_from = {1: ("sc", 0, 1), 4: ("sc", 0, 3), PH: ("sc", 1, 1)}
            for g in range(GPT):
                H = g // GPH
                group(H % 3, g % GPH, *flat_group(H, g % GPH))
                for st in after_group(g, False):
                    step(*st)
                if g % GPH == 0 and H + 1 in scores_from:
                    dve.wait_ge(a_free, AN[scores_from[H + 1]] + 1)
                top_part(TOP_AT.get(g % GPH), H + 1, (H + 1) % 3, static_scores(H + 1))
            start_tile(1)
            dve.wait_ge(up_used, GPT)
            nc.vector.tensor_copy(YS[0], y[:, :]).then_inc(y_out, 1)
            finish(0, YS[0])
            dve.wait_ge(a_free, AN[("sc", 1, 3)] + 1)
            with dve.Fori(LOOP_LO, LOOP_HI) as m:
                for j in range(3):
                    for k in range(GPH):
                        group((2 + j) % 3, k, *loop_group(m, j, k))
                        top_part(TOP_AT.get(k), m * 3 + (3 + j), (3 + j) % 3,
                                 SALL[1][:, bass.ds((m * 3 + (3 + j - PH)) * (2 * NKEY), 2 * NKEY)])
            for H in (2 * PH - 2, 2 * PH - 1):
                for k in range(GPH):
                    group(H % 3, k, *flat_group(H, k))
                    if H < 2 * PH - 1:
                        top_part(TOP_AT.get(k), H + 1, (H + 1) % 3, static_scores(H + 1))
            finish(1, y[:, :])

        @block.tensor
        def _(pe):
            def v_job(key):
                n = VN[key]
                if n >= 2:
                    pe.wait_ge(v_free, n - 1)
                return vb[n % 2]

            def a_job(key):
                n = AN[key]
                if n >= 2:
                    pe.wait_ge(a_free, n - 1)
                return ab[n % 2]

            def weights(name, b):
                n = BN[(name, b)]
                pe.wait_ge(w_full[n % W_SLOTS], 16 * (n // W_SLOTS + 1))
                return wblk(name, b)

            def transposes(key, rows, half):
                bank = v_job(key)
                for c in range(4):
                    k = 4 * half + c
                    ins = nc.tensor.transpose(bank[:, c * P:(c + 1) * P], rows[:, k * P:(k + 1) * P], ident[:, :])
                ins.then_inc(v_full, 1)

            def product(bank, lo, n, lhs, rhs, chunks=KC):
                for k in range(chunks):
                    ins = nc.tensor.matmul(bank[:, lo:lo + n], lhs(k), rhs(k), start=(k == 0), stop=(k == chunks - 1))
                return ins

            def split_product(bank, lo, n, a_high, a_low, b_high, b_low):
                for k in range(KC):
                    for p, (a, b) in enumerate(((a_high, b_high), (a_high, b_low), (a_low, b_high))):
                        ins = nc.tensor.matmul(bank[:, lo:lo + n], a(k), b(k),
                                               start=(k == 0 and p == 0), stop=(k == KC - 1 and p == 2))
                return ins

            def h_high(k):
                return HH_r[:, :, k * P:(k + 1) * P]

            def h_low(k):
                return HL_r[:, :, k * P:(k + 1) * P]

            def mem_high(k):
                return MH_r[:, :, k * P:(k + 1) * P]

            def mem_low(k):
                return ML_r[:, :, k * P:(k + 1) * P]

            def half_product(bank, q, high, low, rows):
                w_low, w_high = half_block(q, W_r), WH_r[q % 2]
                pe.wait_ge(low_ready, q + 1)
                for c in range(2):
                    if rows:
                        ins = split_product(bank, c * HC, HC, lambda k: high(k)[:, c, :], lambda k: low(k)[:, c, :],
                                            lambda k: w_high[:, k, :], lambda k: w_low[:, k, :])
                    else:
                        ins = split_product(bank, c * SEQ, SEQ, lambda k: w_high[:, k, c * P:(c + 1) * P],
                                            lambda k: w_low[:, k, c * P:(c + 1) * P], high, low)
                return ins

            def step(name, t, i):
                key = (name, t, i)
                if name == "gains":
                    pe.wait_ge(id_ready, 1)
                    pe.wait_ge(ld_gain, 16 * 5)
                    bank = v_job(key)
                    nc.tensor.transpose(bank[:, 0:32], grow[:, :], ident[0:32, 0:32]).then_inc(v_full, 1)
                elif name == "memT":
                    pe.wait_ge(xs_done, XN[("scale_m", 0, t)])
                    transposes(key, MEM[t], i)
                elif name == "hT":
                    pe.wait_ge(xs_done, XN[("scale_h", t, 0)])
                    transposes(key, V[:, t, :], i)
                elif name == "skT":
                    pe.wait_ge(ld_sk, 32)
                    transposes(key, sk_nat.rearrange("p h x -> p (h x)"), i)
                elif name == "bias":
                    pe.wait_ge(ld_rel, 32)
                    bank = a_job(key)
                    nc.tensor.matmul(bank[0:NH, 0:FDIST], relb[:, :], onehot, start=True, stop=True)\
                        .then_inc(a_full, 1)
                elif name == "mK":
                    pe.wait_ge(ml_ready, 2)
                    half_product(a_job(key), HN[("w_xk", t, i)], mem_high, mem_low, False).then_inc(a_full, 1)
                elif name == "mV":
                    half_product(a_job(key), HN[("w_xv", t, i)], mem_high, mem_low, True).then_inc(a_full, 1)
                elif name == "forget":
                    pe.wait_ge(hl_ready, T + 1)
                    bank = v_job(key)
                    split_product(bank[0:NH, :], 0, SEQ, lambda k: wfh[:, k, :], lambda k: wfl[:, k, :],
                                  h_high, h_low).then_inc(v_full, 1)
                elif name in ("winv", "wina"):
                    pe.wait_ge(hl_ready, T)
                    bank, full = (v_job(key), v_full) if name == "winv" else (a_job(key), a_full)
                    half_product(bank, HN[("w_in", t, i)], h_high, h_low, t in (2, 5)).then_inc(full, 1)
                elif name == "S":
                    if SN[(t, i)] == 0:
                        pe.wait_ge(a_free, AN[("wina", 5, 1)] + 1)
                        pe.wait_ge(v_free, VN[("winv", 5, 0)] + 1)
                        pe.wait_ge(nc_ready, 1)
                    nk = (t + 1) * P
                    bank = v_job(key)
                    lo, c = (i % 2) * HD, i // 2
                    ins = nc.tensor.matmul(bank[:, 0:nk], Q[lo:lo + HD, t, c, :], K[lo:lo + HD, 0:t + 1, c, :],
                                           start=True, stop=i < NH)
                    if i >= NH:
                        ins = nc.tensor.matmul(bank[:, 0:nk], ident[0:NH, i - NH:i - NH + 1].broadcast_to([NH, P]),
                                               small[:, 1, 0:nk], start=False, stop=True)
                    ins.then_inc(v_full, 1)
                elif name == "PT":
                    n = SN[(t, i)]
                    pe.wait_ge(p_ready, n + 1)
                    bank = a_job(key)
                    for j in range(t + 1):
                        ins = nc.tensor.transpose(bank[:, j * P:(j + 1) * P], Pr[:, n % 2, j * P:(j + 1) * P],
                                                  ident[:, :])
                    ins.then_inc(a_full, 1)
                elif name == "O":
                    n = SN[(t, i)]
                    pe.wait_ge(a_free, AN[("PT", t, i)] + 1)
                    if t and i % NH == 0:
                        pe.wait_ge(o_raw, 2 * (t - 1) + i // NH + 1)
                    for j in range(t + 1):
                        ins = nc.tensor.matmul(y[:, i * HD:(i + 1) * HD], PT[:, n % 2, j * P:(j + 1) * P],
                                               V[:, j, i * HD:(i + 1) * HD], start=(j == 0), stop=(j == t))
                    if i % NH == NH - 1:
                        ins.then_inc(o_full, 1)
                elif name == "oT":
                    pe.wait_ge(xs_done, XN[("o_scale", t, 0)])
                    transposes(key, HTpage[t], i)
                elif name == "wout":
                    w = weights("w_out", i)
                    pe.wait_ge(v_free, VN[("oT", t, 1)] + 1)
                    bank = v_job(key)
                    product(bank, 0, BLK, lambda k: HT[t][:, k, :], lambda k: w[:, k, :]).then_inc(v_full, 1)
                elif name == "xT":
                    pe.wait_ge(xs_done, XN[("scale_x", t, 0)])
                    transposes(key, XS, i)
                elif name == "xq":
                    w = weights("w_xq", i)
                    pe.wait_ge(v_free, VN[("xT", t, 1)] + 1)
                    bank = a_job(key)
                    for c in range(4):
                        ins = product(bank, c * P, P, lambda k: w[:, k, c * P:(c + 1) * P], lambda k: HT[t][:, k, :])
                    ins.then_inc(a_full, 1)
                elif name == "xS":
                    pe.wait_ge(a_free, AN[("xq", t, 1)] + 1)
                    bank = a_job(key)
                    product(bank, 0, M, lambda j: XQ[:, 2 * i + j, :], lambda j: KM[:, 2 * i + j, :], 2)\
                        .then_inc(a_full, 1)
                elif name == "xPT":
                    n = t * XH_N + i
                    pe.wait_ge(xp, n + 1)
                    bank = a_job(key)
                    for j in range(2):
                        ins = nc.tensor.transpose(bank[:, j * P:(j + 1) * P], Pr[:, n % 2, j * P:(j + 1) * P],
                                                  ident[:, :])
                    ins.then_inc(a_full, 1)
                elif name == "xO":
                    pe.wait_ge(a_free, AN[("xPT", t, i)] + 1)
                    bank = v_job(key)
                    for c in range(2):
                        cc = i * XHD + c * P
                        ins = product(bank, c * P, P, lambda j: VM[:, j, cc:cc + P],
                                      lambda j: PT[:, i % 2, j * P:(j + 1) * P], 2)
                    ins.then_inc(v_full, 1)
                elif name == "xo":
                    w = weights("w_xo", i)
                    pe.wait_ge(v_free, VN[("xO", t, XH_N - 1)] + 1)
                    bank = v_job(key)
                    product(bank, 0, BLK, lambda k: XQ[:, k, :], lambda k: w[:, k, :]).then_inc(v_full, 1)
                elif name == "pT":
                    pe.wait_ge(xs_done, XN[("scale_p", t, 0)])
                    transposes(key, XS, i)
                elif name == "y_start":
                    pe.wait_ge(v_free, VN[("xo", t, 1)] + 1)
                    y_start(t)
                elif name in ("wq", "wq_first"):
                    if t == 0 and i == 0:
                        w = wq_early
                        pe.wait_ge(ld_early, 16)
                    else:
                        w = weights("w_peer_query", i)
                    pe.wait_ge(v_free, VN[("pT", t, 1)] + 1)
                    bank = a_job(key)
                    for h in block_heads(t, i) if name == "wq" else range(1):
                        c = h - 4 * i
                        ins = product(bank, c * P, P, lambda k: w[:, k, c * P:(c + 1) * P], lambda k: HT[t][:, k, :])
                    ins.then_inc(a_full, 1)
                elif name in ("sc", "sc_first"):
                    quad, lo = i // 2, (i % 2) * HD
                    pe.wait_ge(a_free, AN[("wq" if name == "sc" else "wq_first", t, quad)] + 1)
                    bank = a_job(key)
                    for h in block_heads(t, quad) if name == "sc" else range(1):
                        hh = h - 4 * quad
                        ins = nc.tensor.matmul(bank[:, hh * NKEY:(hh + 1) * NKEY], QR[t][lo:lo + HD, h, :],
                                               skT[lo:lo + HD, h, :], start=True, stop=True)
                    ins.then_inc(a_full, 1)

            def y_start(t):
                for b in range(2):
                    nc.tensor.matmul(y[:, b * BLK:(b + 1) * BLK], ident[:, :], X[t][:, b * BLK:(b + 1) * BLK],
                                     start=True, stop=False)

            def group(g, par, before, last=False):
                pe.wait_ge(diag_done, g + 1)
                for u in range(U):
                    pe.wait_ge(up_in[par * U + u], (before + 1) * 16)
                    for b in range(2):
                        ins = nc.tensor.matmul(y[:, b * BLK:(b + 1) * BLK], diag[:, par, u, :],
                                               UPB[par * U + u][:, b * BLK:(b + 1) * BLK], start=False,
                                               stop=last and u == U - 1)
                ins.then_inc(up_used, 1)

            for st in main:
                step(*st)
            for g in range(GPT):
                group(*flat_group(g // GPH, g % GPH), last=g == GPT - 1)
                for st in after_group(g, True):
                    step(*st)
            pe.wait_ge(y_out, 1)
            y_start(1)
            with pe.Fori(LOOP_LO, LOOP_HI) as m:
                for j in range(3):
                    for k in range(GPH):
                        group(*loop_group(m, j, k))
            for H in (2 * PH - 2, 2 * PH - 1):
                for k in range(GPH):
                    group(*flat_group(H, k), last=H * GPH + k == T * GPT - 1)


INPUTS = ["x", "mem", "norm_mix", "w_in", "b_forget", "rel_bias", "g_moba_out", "g_fox_out", "w_out", "norm_xattn",
          "norm_mem", "w_xq", "w_xk", "w_xv", "w_xo", "norm_ffn", "w_peer_query", "peer_subkeys_1",
          "peer_subkeys_2", "peer_expert_down", "peer_expert_up", "norm_final"]


def kernel(**inputs):
    import concourse.bacc as bacc
    from concourse.bass_utils import run_bass_kernel_spmd as run

    nc = bacc.Bacc("TRN2", target_bir_lowering=False, num_devices=1)
    arrays, aps = {}, {}
    for name in INPUTS:
        arrays[f"in_{name}"] = np.ascontiguousarray(inputs[name])
    arrays["in_bucket_rows"] = bucket_rows()
    for key, a in arrays.items():
        aps[key[3:]] = nc.dram_tensor(key, a.shape, mybir.dt.from_np(a.dtype), kind="ExternalInput").ap()
    out = nc.dram_tensor("out", (1, SEQ, D), mybir.dt.float32, kind="ExternalOutput").ap()
    bias_scratch = nc.dram_tensor("bias_scratch", (NH, P, FDIST), mybir.dt.float32).ap()
    hybrid_layer(nc, aps, out, bias_scratch)
    r = run(nc, [arrays], core_ids=[0])
    return r.results[0]["out"]
```
